# Optimizing a Trainium2 kernel written in Bass

```python
import jax, jax.numpy as jnp
from jax import lax
import numpy as np

D_MODEL = 1024
BATCH = 1
SEQ = 256
DEPTH = 2

GMLP_GROUPS = 8
GMLP_GROUP_DIM = 64
GMLP_WIDTH = GMLP_GROUPS * GMLP_GROUP_DIM
CHUNK = 128
MLA_HEADS = 8
QK_NOPE_DIM = 64
QK_ROPE_DIM = 32
V_HEAD_DIM = 64
Q_LORA_RANK = 384
KV_LORA_RANK = 256
QK_HEAD_DIM = QK_NOPE_DIM + QK_ROPE_DIM
MLA_WIDTH = MLA_HEADS * V_HEAD_DIM
ROPE_THETA = 10000.0
Q_BLOCK = 128
IN_SPLITS = (
    GMLP_WIDTH,
    2 * GMLP_WIDTH,
    2 * GMLP_WIDTH + Q_LORA_RANK,
    2 * GMLP_WIDTH + Q_LORA_RANK + KV_LORA_RANK,
    2 * GMLP_WIDTH + Q_LORA_RANK + KV_LORA_RANK + QK_ROPE_DIM,
    2 * GMLP_WIDTH + Q_LORA_RANK + KV_LORA_RANK + QK_ROPE_DIM + D_MODEL,
)
IN_TOTAL = 2 * GMLP_WIDTH + Q_LORA_RANK + KV_LORA_RANK + QK_ROPE_DIM + 2 * D_MODEL
DENSE_FF = 2752
N_EXPERTS = 8
TOP_K = 2
EXPERT_FF = 3584
MOE_BLOCK = 128
N_DENSE = (DEPTH + 1) // 2
N_MOE = DEPTH // 2
EPS = 1e-6

kernel_name = "hybrid_gmlp_mla_moe_block"

def rms_norm(x, g):
    xf = x.astype(jnp.float32)
    y = xf * lax.rsqrt(jnp.mean(xf * xf, axis=-1, keepdims=True) + EPS)
    return (y * g.astype(jnp.float32)).astype(x.dtype)

def layer_norm(x, g, b):
    xf = x.astype(jnp.float32)
    mu = jnp.mean(xf, axis=-1, keepdims=True)
    xc = xf - mu
    y = xc * lax.rsqrt(jnp.mean(xc * xc, axis=-1, keepdims=True) + EPS)
    return (y * g.astype(jnp.float32) + b.astype(jnp.float32)).astype(x.dtype)

def rope_tables(positions, dtype):
    inv_freq = 1.0 / (ROPE_THETA ** (jnp.arange(0, QK_ROPE_DIM, 2, dtype=jnp.float32) / QK_ROPE_DIM))
    ang = positions.astype(jnp.float32)[..., None] * inv_freq
    return jnp.cos(ang).astype(dtype), jnp.sin(ang).astype(dtype)

def rope(x, cos, sin):
    x1, x2 = jnp.split(x, 2, axis=-1)
    return jnp.concatenate([x1 * cos - x2 * sin, x2 * cos + x1 * sin], axis=-1)

def gmlp_spatial_gating(u, v, ln_g, ln_b, w_s, b_s):
    B, S, _ = u.shape
    u = jax.nn.gelu(u, approximate=False)
    v = layer_norm(jax.nn.gelu(v, approximate=False), ln_g, ln_b)
    vc = v.reshape(B, S // CHUNK, CHUNK, GMLP_GROUPS, GMLP_GROUP_DIM)
    causal = jnp.tril(jnp.ones((CHUNK, CHUNK), dtype=bool))
    ws = jnp.where(causal[None], w_s, jnp.zeros((), w_s.dtype))
    z = jnp.einsum('gts,bcsgd->bctgd', ws, vc) + b_s.T[None, None, :, :, None]
    return u * z.reshape(B, S, GMLP_WIDTH)

def mla_attention(c_q, c_kv, k_rope, cos, sin, q_norm, w_uq, kv_norm, w_ukv):
    B, S, _ = c_q.shape
    q = (rms_norm(c_q, q_norm) @ w_uq).reshape(B, S, MLA_HEADS, QK_HEAD_DIM)
    q_nope, q_pe = jnp.split(q, [QK_NOPE_DIM], axis=-1)
    q_pe = rope(q_pe, cos[:, :, None, :], sin[:, :, None, :])
    kv = (rms_norm(c_kv, kv_norm) @ w_ukv).reshape(B, S, MLA_HEADS, QK_NOPE_DIM + V_HEAD_DIM)
    k_nope, v = jnp.split(kv, [QK_NOPE_DIM], axis=-1)
    k_pe = rope(k_rope, cos, sin)[:, :, None, :]
    q = jnp.concatenate([q_nope, q_pe], axis=-1)
    k = jnp.concatenate([k_nope, jnp.broadcast_to(k_pe, (B, S, MLA_HEADS, QK_ROPE_DIM))], axis=-1)
    scale = QK_HEAD_DIM ** -0.5
    kpos = jnp.arange(S)

    def attend(i):
        q0 = i * Q_BLOCK
        qb = lax.dynamic_slice_in_dim(q, q0, Q_BLOCK, axis=1)
        s = jnp.einsum('bqhd,bkhd->bhqk', qb, k).astype(jnp.float32) * scale
        qpos = q0 + jnp.arange(Q_BLOCK)
        s = jnp.where(kpos[None, :] <= qpos[:, None], s, -jnp.inf)
        p = jax.nn.softmax(s, axis=-1).astype(v.dtype)
        return jnp.einsum('bhqk,bkhd->bqhd', p, v)

    o = lax.map(attend, jnp.arange(S // Q_BLOCK))
    return jnp.moveaxis(o, 0, 1).reshape(B, S, MLA_WIDTH)

def hybrid_mixer(h, cos, sin, w_in, gln_g, gln_b, g_ws, g_bs, q_norm, w_uq, kv_norm, w_ukv,
                 w_branch_a, w_branch_b, w_out):
    proj = h @ w_in
    u, v, c_q, c_kv, k_rope, gate_a, gate_b = jnp.split(proj, IN_SPLITS, axis=-1)
    y_a = gmlp_spatial_gating(u, v, gln_g, gln_b, g_ws, g_bs) @ w_branch_a
    y_b = mla_attention(c_q, c_kv, k_rope, cos, sin, q_norm, w_uq, kv_norm, w_ukv) @ w_branch_b
    merged = jax.nn.sigmoid(gate_a) * y_a + jax.nn.sigmoid(gate_b) * y_b
    return merged @ w_out

def swiglu(h, w_gate, w_up, w_down):
    return (jax.nn.silu(h @ w_gate) * (h @ w_up)) @ w_down

def moe_swiglu(h, w_router, b_router, w1, w3, w2):
    B, S, D = h.shape
    N = B * S
    xt = h.reshape(N, D)
    logits = (xt @ w_router + b_router).astype(jnp.float32)
    top_val, top_idx = lax.top_k(logits, TOP_K)
    gates = jax.nn.softmax(top_val, axis=-1).astype(h.dtype)
    A = N * TOP_K
    flat_e = top_idx.reshape(A).astype(jnp.int32)
    flat_tok = jnp.arange(A, dtype=jnp.int32) // TOP_K
    flat_g = gates.reshape(A)
    order = jnp.argsort(flat_e)
    se, stok, sg = flat_e[order], flat_tok[order], flat_g[order]
    counts = jnp.bincount(flat_e, length=N_EXPERTS).astype(jnp.int32)
    padded = ((counts + MOE_BLOCK - 1) // MOE_BLOCK) * MOE_BLOCK
    start = jnp.cumsum(counts) - counts
    pend = jnp.cumsum(padded)
    pstart = pend - padded
    dest = pstart[se] + (jnp.arange(A, dtype=jnp.int32) - start[se])
    n_blocks = (A + MOE_BLOCK - 1) // MOE_BLOCK + N_EXPERTS
    P = n_blocks * MOE_BLOCK
    buf_tok = jnp.full((P,), N, dtype=jnp.int32).at[dest].set(stok)
    buf_g = jnp.zeros((P,), h.dtype).at[dest].set(sg)
    block_e = jnp.minimum(
        jnp.searchsorted(pend, jnp.arange(n_blocks, dtype=jnp.int32) * MOE_BLOCK, side='right'),
        N_EXPERTS - 1)
    x_pad = jnp.concatenate([xt, jnp.zeros((1, D), h.dtype)], axis=0)

    def run_block(args):
        tok, e = args
        xb = x_pad[tok]
        hb = jax.nn.silu(xb @ w1[e]) * (xb @ w3[e])
        return hb @ w2[e]

    yb = lax.map(run_block, (buf_tok.reshape(n_blocks, MOE_BLOCK), block_e))
    yb = yb.reshape(P, D) * buf_g[:, None]
    out = jnp.zeros((N + 1, D), h.dtype).at[buf_tok].add(yb)[:N]
    return out.reshape(B, S, D)

def setup_inputs(seed: int = 0) -> dict:
    key = jax.random.key(seed)
    ks = iter(jax.random.split(key, 32))
    L, D = DEPTH, D_MODEL

    def nrm(shape, scale):
        return jax.random.normal(next(ks), shape, jnp.float32) * scale

    return {
        "x": nrm((BATCH, SEQ, D), 1.0),
        "c": nrm((BATCH, D), 1.0),
        "positions": jnp.broadcast_to(jnp.arange(SEQ, dtype=jnp.int32)[None, :], (BATCH, SEQ)),
        "ada_w": nrm((L, D, 6 * D), D ** -0.5),
        "ada_b": nrm((L, 6 * D), 0.02),
        "norm_mix_pre": 1.0 + nrm((L, D), 0.05),
        "norm_mix_post": 1.0 + nrm((L, D), 0.05),
        "norm_ffn_pre": 1.0 + nrm((L, D), 0.05),
        "norm_ffn_post": 1.0 + nrm((L, D), 0.05),
        "w_in": nrm((L, D, IN_TOTAL), D ** -0.5),
        "gmlp_ln_g": 1.0 + nrm((L, GMLP_WIDTH), 0.05),
        "gmlp_ln_b": nrm((L, GMLP_WIDTH), 0.02),
        "gmlp_ws": nrm((L, GMLP_GROUPS, CHUNK, CHUNK), CHUNK ** -0.5),
        "gmlp_bs": 1.0 + nrm((L, GMLP_GROUPS, CHUNK), 0.02),
        "mla_q_norm": 1.0 + nrm((L, Q_LORA_RANK), 0.05),
        "mla_w_uq": nrm((L, Q_LORA_RANK, MLA_HEADS * QK_HEAD_DIM), Q_LORA_RANK ** -0.5),
        "mla_kv_norm": 1.0 + nrm((L, KV_LORA_RANK), 0.05),
        "mla_w_ukv": nrm((L, KV_LORA_RANK, MLA_HEADS * (QK_NOPE_DIM + V_HEAD_DIM)), KV_LORA_RANK ** -0.5),
        "w_branch_a": nrm((L, GMLP_WIDTH, D), GMLP_WIDTH ** -0.5),
        "w_branch_b": nrm((L, MLA_WIDTH, D), MLA_WIDTH ** -0.5),
        "w_out": nrm((L, D, D), D ** -0.5),
        "ffn_w_gate": nrm((N_DENSE, D, DENSE_FF), D ** -0.5),
        "ffn_w_up": nrm((N_DENSE, D, DENSE_FF), D ** -0.5),
        "ffn_w_down": nrm((N_DENSE, DENSE_FF, D), DENSE_FF ** -0.5),
        "moe_router": nrm((N_MOE, D, N_EXPERTS), D ** -0.5),
        "moe_router_bias": nrm((N_MOE, N_EXPERTS), 0.01),
        "moe_w1": nrm((N_MOE, N_EXPERTS, D, EXPERT_FF), D ** -0.5),
        "moe_w3": nrm((N_MOE, N_EXPERTS, D, EXPERT_FF), D ** -0.5),
        "moe_w2": nrm((N_MOE, N_EXPERTS, EXPERT_FF, D), EXPERT_FF ** -0.5),
    }

def reference(x, c, positions, ada_w, ada_b, norm_mix_pre, norm_mix_post, norm_ffn_pre, norm_ffn_post,
              w_in, gmlp_ln_g, gmlp_ln_b, gmlp_ws, gmlp_bs, mla_q_norm, mla_w_uq, mla_kv_norm, mla_w_ukv,
              w_branch_a, w_branch_b, w_out, ffn_w_gate, ffn_w_up, ffn_w_down,
              moe_router, moe_router_bias, moe_w1, moe_w3, moe_w2):
    cos, sin = rope_tables(positions, x.dtype)
    c_act = jax.nn.silu(c)
    for l in range(DEPTH):
        mod = (c_act @ ada_w[l] + ada_b[l])[:, None, :]
        sh_m, sc_m, g_m, sh_f, sc_f, g_f = jnp.split(mod, 6, axis=-1)
        h = rms_norm(x, norm_mix_pre[l]) * (1 + sc_m) + sh_m
        y = hybrid_mixer(h, cos, sin, w_in[l], gmlp_ln_g[l], gmlp_ln_b[l], gmlp_ws[l], gmlp_bs[l],
                         mla_q_norm[l], mla_w_uq[l], mla_kv_norm[l], mla_w_ukv[l],
                         w_branch_a[l], w_branch_b[l], w_out[l])
        x = x + g_m * rms_norm(y, norm_mix_post[l])
        h = rms_norm(x, norm_ffn_pre[l]) * (1 + sc_f) + sh_f
        if l % 2 == 0:
            j = l // 2
            y = swiglu(h, ffn_w_gate[j], ffn_w_up[j], ffn_w_down[j])
        else:
            j = l // 2
            y = moe_swiglu(h, moe_router[j], moe_router_bias[j], moe_w1[j], moe_w3[j], moe_w2[j])
        x = x + g_f * rms_norm(y, norm_ffn_post[l])
    return x


_drawn_inputs = setup_inputs


def setup_inputs(seed=0):
    import zlib

    import numpy as np

    out = dict(_drawn_inputs(seed))
    spreads = {}
    factors = {'mla_q_norm': 5.888, 'gmlp_ln_b': 2.67}
    for name, (base, spread) in spreads.items():
        noise = np.random.default_rng([zlib.crc32(name.encode()), seed]).standard_normal(out[name].shape)
        drawn = base * np.exp(spread * noise) if base else spread * noise
        out[name] = __import__('jax').numpy.asarray(drawn.astype(out[name].dtype))
    for name, factor in factors.items():
        out[name] = (out[name] * factor).astype(out[name].dtype)
    return out
```

```python
from contextlib import ExitStack

import numpy as np
import concourse.bass as bass
from concourse import mybir

P = 128
D = 1024
SEQ = 256
T = SEQ // P
K = D // P
L = 2
GROUPS, GDIM = 8, 64
GW = GROUPS * GDIM
HEADS, NOPE, ROPE, VD = 8, 64, 32, 64
QKD = NOPE + ROPE
QR, KVR = 384, 256
QC, KC = QR // P, KVR // P
LATC = QC + KC
HALF = ROPE // 2
THETA = 10000.0
FF_DENSE = 2752
FT = (FF_DENSE + P - 1) // P
FG = FT // 2
LASTROW = (FT * P - FF_DENSE)
EXPERTS = 8
FF_EXP = 3584
GRP = 512
NG = FF_EXP // GRP
SPARE = 3
ITEMS = EXPERTS + SPARE
CH = 2048
NRAW, NSPLIT = 6, 3
PER_ITEM = 6 * NG
EPS = 1e-6
NEG = -1.0e30
LAG_SUM, LAG_USE = 3, 6

f32 = mybir.dt.float32
f32r = mybir.dt.float32r
i32 = mybir.dt.int32
ALU = mybir.AluOpType
ACT = mybir.ActivationFunctionType
AX = mybir.AxisListType.X

SH_M, SC_M, G_M, SH_F, SC_F, G_F = range(6)

COL_C = 0
COL_ADA = COL_C + K
COL_NORM = COL_ADA + L * 6 * K
COL_QN = COL_NORM + L * 2 * K
COL_KVN = COL_QN + L * QC
COL_BS = COL_KVN + L * KC
COL_WR = COL_BS + L * GROUPS
COLS = COL_WR + K * EXPERTS


def mixer_chunks(l):
    out = [(f"cq{h}", "w_cq", (l, h), 4 * QR) for h in range(2)]
    out += [(f"kr{h}", "w_kr", (l, h), 4 * (KVR + ROPE)) for h in range(2)]
    out += [(f"v{h}", "w_v", (l, h), 4 * GW) for h in range(2)]
    out += [(f"u{h}", "w_u", (l, h), 4 * GW) for h in range(2)]
    out += [(f"uq{h}", "w_uq", (l, h), QC * QR) for h in range(2)]
    out += [("ukv", "w_ukv", (l, 0), CH)]
    for j in range(4):
        out += [(f"ga{j}", "w_ga", (l, j), CH), (f"gb{j}", "w_gb", (l, j), CH), (f"ab{j}", "w_ab", (l, j), CH)]
    out += [(f"wo{j}", "w_o", (l, j), CH) for j in range(4)]
    return [((f"m{l}." + n), t, i, e) for n, t, i, e in out]


def ffn_chunks():
    out = []
    for j in range(FG):
        out += [(f"fg{j}", "w_fg", (0, j), CH), (f"fu{j}", "w_fu", (0, j), CH)]
        if j:
            out.append((f"fd{j - 1}", "w_fd", (0, j - 1), CH))
    return out + [(f"fd{FG - 1}", "w_fd", (0, FG - 1), CH)]


WEIGHTS = mixer_chunks(0) + ffn_chunks() + mixer_chunks(1)
CHUNK = {name: s for s, (name, _, _, _) in enumerate(WEIGHTS)}
NW = len(WEIGHTS)
M0, F0, M1 = 0, len(mixer_chunks(0)), len(mixer_chunks(0)) + len(ffn_chunks())
ADA_FIRST = [(0, SH_M), (0, SC_M)]
ADA_AT = [(0, G_M, M0), (0, SH_F, M0 + 9), (0, SC_F, M0 + 16),
          (1, SH_M, F0), (1, SC_M, F0 + 6), (0, G_F, F0 + 12), (1, G_M, F0 + 21),
          (1, SH_F, M1), (1, SC_F, M1 + 6), (1, G_F, M1 + 12)]
ADA = ADA_FIRST + [(l, v) for l, v, _ in ADA_AT]


def stream():
    out = [("ada", a, q) for a in range(len(ADA_FIRST)) for q in range(4)]
    for s in range(NW):
        for a, (_, _, at) in enumerate(ADA_AT):
            if at <= s < at + 4:
                out.append(("ada", len(ADA_FIRST) + a, s - at))
        out.append(("w", s, 0))
    return out


STREAM = stream()
RAW_OF = {(kind, n, q): r for r, (kind, n, q) in enumerate(STREAM)}
NR = len(STREAM)


def ada_sums():
    out = []
    for a, (_, v, at) in enumerate(ADA_AT, len(ADA_FIRST)):
        for half in range(2 if v in (G_M, G_F) else 1):
            out.append((a, half, at + LAG_SUM * (1 + half), at + LAG_USE + LAG_SUM * half))
    return out


SUMS = ada_sums()


def spot(kind, g, half=1, first=False):
    if kind == "w2":
        c = 6 * (g + 1) + 4 + half
    else:
        c = 6 * g + (0 if kind == "w1" else 2) + half
    return c if first and c < 4 else c - 2


def item_order(first):
    out = []
    for g in range(NG):
        out += [(spot(kind, g, h, first), kind, g, h, False) for kind in ("w1", "w3") for h in range(2)]
        if g:
            out += [(spot("w2", g - 1, h), "w2", g - 1, h, False) for h in range(2)]
        elif not first:
            out += [(spot("w2", -1, h), "w2", NG - 1, h, True) for h in range(2)]
    return out


LAST = [(PER_ITEM - 2 + h, "w2", NG - 1, h, False) for h in range(2)]
HS = [1024 + 512 * (g % 2 if g < NG - 1 else 2) for g in range(NG)]


def build(nc, A, out):
    with ExitStack() as ctx:
        def sb(name, shape, dt=f32):
            return ctx.enter_context(nc.sbuf_tensor(name, shape, dt))

        def sem(name):
            return ctx.enter_context(nc.semaphore(name))

        raw = sb("raw", [P, NRAW, CH])
        hi = sb("hi", [P, NSPLIT, CH], f32r)
        lo = sb("lo", [P, NSPLIT, CH], f32r)
        x = sb("x_tok", [P, T, D])
        r2 = sb("r2", [P, T * D])
        r3 = sb("r3", [P, T * (HEADS + 1) * QKD + T * HEADS * QKD])
        r4 = sb("r4", [P, 4 * 512])
        r5 = sb("r5", [P, T * HEADS * VD])
        r6 = sb("r6", [P, 2 * HEADS * SEQ])
        r7 = sb("r7", [P, D])
        gate_m = sb("gate_m", [P, D])
        acc = sb("ada_acc", [P, D])
        hTh, hTl = (sb(n, [P, K, SEQ], f32r) for n in ("hT_hi", "hT_lo"))
        bTh, bTl = (sb(n, [P, K, SEQ], f32r) for n in ("bT_hi", "bT_lo"))
        cols = sb("cols", [P, COLS])
        silu_c = sb("silu_c", [P, K])
        AB = sb("scale_shift", [P, 2 * L, 2, K])
        ident = sb("ident", [P, P])
        ones = sb("ones", [P, P])
        before = sb("before", [P, P])
        mask = sb("mask", [P, 2 * P])
        slots_i, slots = sb("slots_i", [P, P], i32), sb("slots", [P, P])
        pos_i, posf = sb("pos_i", [P, T], i32), sb("posf", [P, T])
        inv = sb("inv_freq", [P, HALF])
        cosT, sinT, ang = (sb(n, [P, T, HALF]) for n in ("cos", "sin", "angle"))
        ms, rstd = sb("mean_sq", [P, 4]), sb("rstd", [P, 4])
        bn, mv = sb("bn", [P, T, 6]), sb("mean_var", [P, T, 2])
        small = sb("small", [P, 4])
        mx, nmx = sb("mx", [P, 6, 4]), sb("neg_max", [P, 6, 4])
        psum_p, rinv = sb("sum_p", [P, 6, 4]), sb("rinv", [P, T, HEADS])
        rope_t = sb("rope_t", [P, 2, T * (HEADS + 1) * HALF])
        lt_mask = sb("lt_mask", [P, EXPERTS, EXPERTS])
        rb = sb("router_bias", [P, EXPERTS])
        eidx = sb("expert_idx", [P, EXPERTS])
        eidx_i = sb("expert_idx_i", [P, EXPERTS], i32)
        pos_tab, gate_tab = (sb(n, [P, T, ITEMS]) for n in ("pos_tab", "gate_tab"))
        pg = sb("pg", [P, 2, T])
        info_f, info = sb("info_f", [P, ITEMS + 1]), sb("info", [P, ITEMS + 1], i32)
        ps = ctx.enter_context(nc.psum_tensor("ps", [P, 8, 512], f32))

        xn = r2[:, :].rearrange("p (t d) -> p t d", t=T)
        y_sb = xn
        v_g = r2[:, 0:T * GW].rearrange("p (t d) -> p t d", t=T)
        u_g = r2[:, T * GW:2 * T * GW].rearrange("p (t d) -> p t d", t=T)
        hf = r3[:, 0:K * SEQ].rearrange("p (k s) -> p k s", k=K)
        NQ = T * (HEADS + 1) * QKD
        qk = r3[:, 0:NQ].rearrange("p (t h d) -> p t h d", t=T, h=HEADS + 1)
        k_tok = r3[:, NQ:NQ + T * HEADS * QKD].rearrange("p (t h d) -> p t h d", t=T, h=HEADS)
        pT = r3[:, 0:4 * 512].rearrange("p (u s) -> p u s", u=4)
        lat = r4[:, 0:T * LATC * P].rearrange("p (t d) -> p t d", t=T)
        S = r4[:, :].rearrange("p (u s) -> p u s", u=4)
        v_tok = r5[:, :].rearrange("p (t d) -> p t d", t=T)
        qT = r6[0:QKD, 0:HEADS * SEQ].rearrange("p (h s) -> p h s", h=HEADS)
        kT = r6[0:QKD, HEADS * SEQ:2 * HEADS * SEQ].rearrange("p (h s) -> p h s", h=HEADS)
        ln_g, ln_b = r6[:, HEADS * SEQ:HEADS * SEQ + GW], r6[:, HEADS * SEQ + GW:HEADS * SEQ + 2 * GW]
        o_tok = r6[:, 0:T * GW].rearrange("p (t d) -> p t d", t=T)
        merged = r6[:, HEADS * SEQ:2 * HEADS * SEQ].rearrange("p (k s) -> p k s", k=K)
        y_exp = r6[:, 0:T * D].rearrange("p (t d) -> p t d", t=T)
        ws = r7[:, :].rearrange("p (g t) -> p g t", g=GROUPS)
        gate_f = r7
        cact = silu_c

        def col(at, n=1):
            return cols[:, at:at + n]

        consts_in, small_in = sem("consts_in"), sem("small_in")
        x_in = sem("x_in")
        raw_full = [sem(f"raw_full{i}") for i in range(NRAW)]
        hi_done = sem("hi_done")
        raw_done = sem("raw_done")
        used = sem("used")
        ws_in, ln_in, post_m_in, post_f_in = (sem(n) for n in ("ws_in", "ln_in", "post_m_in", "post_f_in"))
        pool_setup, ws_masked = sem("pool_setup"), sem("ws_masked")
        cact_ready = sem("cact_ready")
        ada_acc, ada_full, ada_used = sem("ada_acc"), sem("ada_full"), sem("ada_used")
        ang_ready, rope_ready = sem("ang_ready"), sem("rope_ready")
        var_ready, rstd_ready = sem("var_ready"), sem("rstd_ready")
        xn_ready, xt_full = sem("xn_ready"), sem("xt_full")
        hf_ready, hth_ready, ht_ready = sem("hf_ready"), sem("hth_ready"), sem("ht_ready")
        lat_copied, vu_done, lat_ready, latT_full = (sem(n) for n in ("lat_copied", "vu_done", "lat_ready", "latT_full"))
        latTh_ready, latT_ready = sem("latTh_ready"), sem("latT_ready")
        attn_copied, qk_ready = sem("attn_copied"), sem("qk_ready")
        qT_full, kT_full, qT_copied, kT_copied = (sem(n) for n in ("qT_full", "kT_full", "qT_copied", "kT_copied"))
        vn_ready, z_full, uz_ready = sem("vn_ready"), sem("z_full"), sem("uz_ready")
        sc_full, s_ready, nmx_ready, p_ready = (sem(n) for n in ("sc_full", "s_ready", "nmx_ready", "p_ready"))
        pT_full, pT_copied, o_full, o_ready = (sem(n) for n in ("pT_full", "pT_copied", "o_full", "o_ready"))
        brT_full, brTh_ready, brT_ready = sem("brT_full"), sem("brTh_ready"), sem("brT_ready")
        sig_done, mg_done, mth_ready, mt_ready = (sem(n) for n in ("sig_done", "mg_done", "mth_ready", "mt_ready"))
        y_copied, x_done = sem("y_copied"), sem("x_done")
        silu_done, hb_done, hbh_ready, hb_ready = (sem(n) for n in ("silu_done", "hb_done", "hbh_ready", "hb_ready"))
        router_full, ex_in, ex_done, sel_ready, count_full, route_ready = (
            sem(n) for n in ("router_full", "ex_in", "ex_done", "sel_ready", "count_full", "route_ready"))
        m_pos, m_gath, m_xf, m_xh, m_x = (sem(n) for n in ("m_pos", "m_gath", "m_xf", "m_xh", "m_x"))
        m_gt, m_gtc, m_silu, m_hb, m_t, m_hh, m_h = (sem(n) for n in ("m_gt", "m_gtc", "m_silu", "m_hb", "m_t", "m_hh", "m_h"))
        m_yc, m_sc, m_acc = sem("m_yc"), sem("m_sc"), sem("m_acc")
        out_done = sem("out_done")
        v_step, v_loop = sem("v_step"), sem("v_loop")
        p_step = sem("p_step")
        a_step = sem("a_step")

        block = ctx.enter_context(nc.Block())

        @block.sync
        def _(sp):
            sp.dma_start(cols[:, :], A["cols"]).then_inc(consts_in, 16)
            sp.dma_start(x[:, :, :], A["x"].rearrange("b (t p) d -> p (b t) d", p=P)).then_inc(x_in, 16)
            for r, (kind, n, q) in enumerate(STREAM):
                if r >= NRAW:
                    sp.wait_ge(raw_done, r - NRAW + 1)
                if kind == "ada":
                    l, v = ADA[n]
                    src, e = A["w_ada"][l, v, q], CH
                else:
                    _, t, (a, b), e = WEIGHTS[n]
                    src = A[t][a, b]
                sp.dma_start(raw[:, r % NRAW, 0:e], src).then_inc(raw_full[r % NRAW], 16)

            def item_loads(i, chunks, expert):
                for c, kind, g, half, before_ in chunks:
                    sp.wait_ge(raw_done, i * PER_ITEM + (NR + c - NRAW + 1))
                    e = expert - 1 if before_ else expert
                    src = A["moe_" + kind]
                    src = src[e, g, half] if isinstance(e, int) else \
                        src[bass.ds(e, 1), g, half, :, :].rearrange("e p n -> p (e n)")
                    slot = (NR + c) % NRAW
                    sp.dma_start(raw[:, slot, :], src).then_inc(raw_full[slot], 16)

            item_loads(0, item_order(True), 0)
            with sp.Fori(1, EXPERTS) as i:
                item_loads(i, item_order(False), i)
            item_loads(EXPERTS - 1, LAST, EXPERTS - 1)
            sp.wait_ge(route_ready, 1)
            spare = sp.value_load(info[0:1, ITEMS:ITEMS + 1], min_val=0, max_val=SPARE)
            with sp.Fori(EXPERTS, ITEMS) as i:
                with sp.If(i < spare + EXPERTS):
                    expert = sp.value_load(info[0:1, bass.ds(i, 1)], min_val=0, max_val=EXPERTS - 1)
                    item_loads(i, item_order(True) + LAST, expert)
            for t in range(T):
                sp.wait_ge(x_done, 2 * L * T - T + 1 + t)
                sp.dma_start(out[0, t * P:(t + 1) * P, :], x[:, t, :]).then_inc(out_done, 16)
            sp.wait_ge(out_done, 16 * T)

        @block.gpsimd
        def _(pool):
            pool.dma_start(pos_i[:, :], A["positions"]).then_inc(small_in, 16)
            pool.dma_start(rb[:, :], A["router_bias"].to_broadcast([P, EXPERTS])).then_inc(small_in, 16)

            def load_ws(l):
                pool.dma_start(r7[:, :], A["ws"][l]).then_inc(ws_in, 16)

            def load_ln(l):
                pool.dma_start(ln_g, A["ln_g"][l:l + 1].to_broadcast([P, GW])).then_inc(ln_in, 16)
                pool.dma_start(ln_b, A["ln_b"][l:l + 1].to_broadcast([P, GW])).then_inc(ln_in, 16)

            def load_post(dst, name, l, s):
                pool.dma_start(dst[:, :], A[name][l:l + 1].to_broadcast([P, D])).then_inc(s, 16)

            def mask_ws(l):
                pool.wait_ge(ws_in, 16 * (l + 1))
                pool.affine_select(out=ws, in_=ws, compare_op=ALU.is_ge, fill=0.0, base=0,
                                   pattern=[[0, GROUPS], [1, P]], channel_multiplier=-1).then_inc(ws_masked, 1)

            load_ws(0)
            load_ln(0)
            load_post(gate_m, "post_m", 0, post_m_in)
            pool.memset(ident[:, :], 0.0).then_inc(p_step, 1)
            pool.memset(ones[:, :], 1.0).then_inc(p_step, 1)
            pool.memset(before[:, :], 1.0).then_inc(p_step, 1)
            pool.memset(mask[:, :], 0.0).then_inc(p_step, 1)
            pool.memset(lt_mask[:, :, :], 1.0).then_inc(p_step, 1)
            for f in range(HALF):
                value = float(np.float32(1.0) / np.float32(THETA) ** np.float32(2.0 * f / ROPE))
                pool.memset(inv[:, f:f + 1], value).then_inc(p_step, 1)
            pool.iota(slots_i[:, :], pattern=[[1, P]], base=0, channel_multiplier=0).then_inc(p_step, 1)
            pool.iota(eidx_i[:, :], pattern=[[1, EXPERTS]], base=0, channel_multiplier=0).then_inc(p_step, 1)
            pool.wait_ge(p_step, 7 + HALF)
            pool.affine_select(out=ident[:, :], in_=ident[:, :], compare_op=ALU.not_equal, fill=1.0, base=0,
                               pattern=[[-1, P]], channel_multiplier=1).then_inc(pool_setup, 1)
            pool.affine_select(out=before[:, :], in_=before[:, :], compare_op=ALU.is_gt, fill=0.0, base=0,
                               pattern=[[1, P]], channel_multiplier=-1).then_inc(pool_setup, 1)
            pool.affine_select(out=mask[:, P:2 * P], in_=mask[:, P:2 * P], compare_op=ALU.is_ge, fill=NEG, base=0,
                               pattern=[[-1, P]], channel_multiplier=1).then_inc(pool_setup, 1)
            pool.affine_select(out=lt_mask[:, :, :], in_=lt_mask[:, :, :], compare_op=ALU.is_gt, fill=0.0, base=0,
                               pattern=[[1, EXPERTS], [-1, EXPERTS]], channel_multiplier=0).then_inc(pool_setup, 1)
            pool.tensor_copy(slots[:, :], slots_i[:, :]).then_inc(pool_setup, 1)
            pool.tensor_copy(eidx[:, :], eidx_i[:, :]).then_inc(pool_setup, 1)
            mask_ws(0)
            pool.wait_ge(z_full, T)
            load_post(gate_f, "post_f", 0, post_f_in)
            pool.wait_ge(x_done, T)
            load_post(gate_m, "post_m", 1, post_m_in)
            pool.wait_ge(x_done, 2 * T)
            load_ws(1)
            load_ln(1)
            mask_ws(1)
            pool.wait_ge(z_full, 2 * T)
            load_post(gate_f, "post_f", 1, post_f_in)

        @block.scalar
        def _(act):
            done = [0]

            def hi_part(s):
                r = RAW_OF["w", s, 0]
                e = WEIGHTS[s][3]
                act.wait_ge(raw_full[r % NRAW], 16 * (r // NRAW + 1))
                if s >= NSPLIT:
                    act.wait_ge(used, s - NSPLIT + 1)
                act.activation(hi[:, s % NSPLIT, 0:e], raw[:, r % NRAW, 0:e], ACT.Copy).then_inc(hi_done, 1)

            def upto(name, ahead=2):
                while done[0] < min(CHUNK[name] + ahead + 1, NW):
                    hi_part(done[0])
                    done[0] += 1

            def need(name):
                act.wait_ge(used, CHUNK[name] + 1)

            roots = [0]

            def root(n):
                roots[0] += 1
                act.wait_ge(var_ready, roots[0])
                act.activation(rstd[:, 0:n], ms[:, 0:n], ACT.Sqrt).then_inc(rstd_ready, 1)

            def h_hi(n):
                for b in range(4):
                    act.wait_ge(hf_ready, 4 * n + b + 1)
                    act.activation(hTh[:, 2 * b:2 * b + 2, :], hf[:, 2 * b:2 * b + 2, :], ACT.Copy).then_inc(hth_ready, 1)

            act.wait_ge(consts_in, 16)
            act.activation(cact[:, :], cols[:, COL_C:COL_C + K], ACT.Silu).then_inc(cact_ready, 1)
            act.wait_ge(ang_ready, 1)
            act.activation(cosT[:, :, :], cosT[:, :, :], ACT.Sin)
            act.activation(sinT[:, :, :], sinT[:, :, :], ACT.Sin).then_inc(rope_ready, 1)

            def mixer(l):
                root(T)
                upto(f"m{l}.cq0", 1)
                h_hi(2 * l)
                upto(f"m{l}.cq1")
                need(f"m{l}.cq1")
                for t in range(T):
                    act.activation(lat[:, t, 0:QR], ps[:, 4 + t, 0:QR], ACT.Copy).then_inc(lat_copied, 1)
                upto(f"m{l}.kr1")
                need(f"m{l}.kr1")
                for t in range(T):
                    bank = [6, 0][t]
                    act.activation(lat[:, t, QR:QR + KVR], ps[:, bank, 0:KVR], ACT.Copy)
                    act.activation(qk[:, t, HEADS, NOPE:QKD], ps[:, bank, KVR:KVR + ROPE], ACT.Copy).then_inc(lat_copied, 1)
                root(2 * T)
                upto(f"m{l}.v1")
                need(f"m{l}.v1")
                for t in range(T):
                    act.activation(v_g[:, t, :], ps[:, 1 + t, :], ACT.Gelu).then_inc(vu_done, 1)
                for kk in range(LATC):
                    act.wait_ge(latT_full, 3 * l + kk // 2 + 1)
                    at = COL_QN + l * QC + kk if kk < QC else COL_KVN + l * KC + kk - QC
                    act.activation(bTh[:, kk, :], ps[:, [5, 6, 0][kk // 2], (kk % 2) * SEQ:(kk % 2 + 1) * SEQ],
                                   ACT.Identity, scale=col(at)).then_inc(latTh_ready, 1)
                root(T)
                upto(f"m{l}.u1")
                need(f"m{l}.u1")
                for t in range(T):
                    act.activation(u_g[:, t, :], ps[:, 3 + t, :], ACT.Gelu).then_inc(vu_done, 1)
                for h in range(2):
                    upto(f"m{l}.uq{h}")
                    need(f"m{l}.uq{h}")
                    for t in range(T):
                        act.activation(qk[:, t, 4 * h:4 * h + 4, :],
                                       ps[:, [5, 6, 0, 1][2 * h + t], 0:QR].rearrange("p (h d) -> p h d", h=4),
                                       ACT.Copy).then_inc(attn_copied, 1)
                upto(f"m{l}.ukv")
                need(f"m{l}.ukv")
                for t in range(T):
                    act.activation(k_tok[:, t, :, 0:NOPE], ps[:, 2 + t, :].rearrange("p (h d) -> p h d", h=HEADS),
                                   ACT.Copy).then_inc(attn_copied, 1)
                for t in range(T):
                    act.activation(v_tok[:, t, :], ps[:, 4 + t, :], ACT.Copy).then_inc(attn_copied, 1)
                for j in range(4):
                    act.wait_ge(qT_full, 4 * l + j + 1)
                    act.activation(qT[:, 2 * j:2 * j + 2, :],
                                   ps[0:QKD, [6, 0, 1, 2][j], :].rearrange("p (h s) -> p h s", h=2),
                                   ACT.Copy).then_inc(qT_copied, 1)

                def exps(u):
                    heads, keys = (4, P) if u < 2 else (2, SEQ)
                    act.wait_ge(nmx_ready, 6 * l + u + 1)
                    for h in range(heads):
                        m = act.activation(S[:, u % 4, h * keys:(h + 1) * keys], S[:, u % 4, h * keys:(h + 1) * keys],
                                           ACT.Exp, bias=nmx[:, u, h:h + 1], scale=QKD ** -0.5,
                                           accum_out=psum_p[:, u, h:h + 1])
                    m.then_inc(p_ready, 1)

                def copy_pT(u):
                    act.wait_ge(pT_full, 6 * l + u + 1)
                    if u >= 4:
                        act.wait_ge(o_full, T * l + 1)
                    act.activation(pT[:, u % 4, :], ps[:, 1 + u, :], ACT.Copy).then_inc(pT_copied, 1)

                for step, u in ((exps, 0), (exps, 1), (copy_pT, 0), (exps, 2), (copy_pT, 1), (exps, 3), (copy_pT, 2),
                                (copy_pT, 3), (exps, 4), (exps, 5), (copy_pT, 4), (copy_pT, 5)):
                    step(u)
                for i in range(2 * T):
                    t = i % T
                    act.wait_ge(brT_full, 4 * l + i + 1)
                    act.activation(bTh[:, 4 * (i // T):4 * (i // T) + 4, t * P:(t + 1) * P],
                                   ps[:, [4, 5, 6, 0][i], :].rearrange("p (c s) -> p c s", c=4),
                                   ACT.Copy).then_inc(brTh_ready, 1)
                for j in range(4):
                    upto(f"m{l}.gb{j}")
                    need(f"m{l}.gb{j}")
                    for m in range(2):
                        mm = 2 * j + m
                        if mm >= 4:
                            act.wait_ge(mg_done, 8 * l + mm - 3)
                        act.activation(S[:, mm % 4, :], ps[:, 1 + m, :], ACT.Sigmoid).then_inc(sig_done, 1)
                    upto(f"m{l}.ab{j}")
                act.wait_ge(mg_done, 8 * l + 8)
                for h in range(2):
                    act.activation(hTh[:, 4 * h:4 * h + 4, :], merged[:, 4 * h:4 * h + 4, :], ACT.Copy).then_inc(mth_ready, 1)
                upto(f"m{l}.wo3")
                need(f"m{l}.wo3")
                for t in range(T):
                    act.activation(y_sb[:, t, :].rearrange("p (c s) -> p c s", c=2), ps[:, 2 * t:2 * t + 2, :], ACT.Copy).then_inc(y_copied, 1)
                root(T)

            def ffn():
                root(T)
                upto("fg0", 1)
                h_hi(1)
                for j in range(FG):
                    upto(f"fu{j}")
                    need(f"fu{j}")
                    for i in (2 * j, 2 * j + 1):
                        if i >= 4:
                            act.wait_ge(hb_ready, i - 3)
                        act.activation(r4[:, (i % 4) * SEQ:(i % 4 + 1) * SEQ], ps[:, i % 3, 0:SEQ], ACT.Silu).then_inc(silu_done, 1)
                    for i in (2 * j, 2 * j + 1):
                        act.wait_ge(hb_done, i + 1)
                        if i >= K:
                            act.wait_ge(used, CHUNK[f"fd{(i - K) // 2}"] + 1)
                        act.activation(bTh[:, i % K, :], r4[:, (i % 4) * SEQ:(i % 4 + 1) * SEQ], ACT.Copy).then_inc(hbh_ready, 1)
                upto(f"fd{FG - 1}")
                need(f"fd{FG - 1}")
                for t in range(T):
                    act.activation(y_sb[:, t, :].rearrange("p (c s) -> p c s", c=2), ps[:, 3 + 2 * t:5 + 2 * t, :], ACT.Copy).then_inc(y_copied, 1)
                root(T)

            mixer(0)
            ffn()
            mixer(1)

            root(T)
            h_hi(3)
            act.wait_ge(ex_in, 1)
            act.activation(r4[:, 512:512 + T * EXPERTS], r4[:, 512:512 + T * EXPERTS], ACT.Exp).then_inc(ex_done, 1)

            def item_hi(i, lo_c, hi_c):
                for c in range(lo_c, hi_c):
                    slot, s = (NR + c) % NRAW, (NW + c) % NSPLIT
                    act.wait_ge(raw_full[slot], i * (16 * PER_ITEM // NRAW) + 16 * ((NR + c) // NRAW + 1))
                    act.wait_ge(used, i * PER_ITEM + (NW + c - NSPLIT + 1))
                    act.activation(hi[:, s, :], raw[:, slot, :], ACT.Copy).then_inc(hi_done, 1)

            def gather_hi(i, par, h):
                act.wait_ge(m_xf, i * 2 + h + 1)
                act.activation(hTh[:, 4 * h:4 * h + 4, par * P:(par + 1) * P],
                               r3[:, 512 * h:512 * h + 512].rearrange("p (k s) -> p k s", k=4), ACT.Copy).then_inc(m_xh, 1)

            def hidden_hi(i, g):
                act.wait_ge(m_t, i * NG + g + 1)
                act.activation(bTh[:, 0:4, 0:P], ps[:, 6, :].rearrange("p (c s) -> p c s", c=4), ACT.Copy).then_inc(m_hh, 1)

            def copy_y(i, last):
                act.wait_ge(used, i * PER_ITEM + (NW + last + 1))
                act.activation(r5[:, :].rearrange("p (c s) -> p c s", c=2), ps[:, 4:6, :], ACT.Copy).then_inc(m_yc, 1)

            def item(i, par, first, ahead):
                if first:
                    for h in range(2):
                        gather_hi(i, par, h)
                    item_hi(i, 0, 2)
                at = [2 if first else 0]

                def upto_c(c):
                    item_hi(i, at[0], c + 1)
                    at[0] = max(at[0], c + 1)

                for g in range(NG):
                    c = spot("w1", g, 1, first)
                    upto_c(min(c + 2, PER_ITEM - 1))
                    if g == 1 and not first:
                        copy_y(i - 1, spot("w2", NG - 1))
                    act.wait_ge(used, i * PER_ITEM + (NW + c + 1))
                    act.activation(r3[:, HS[g]:HS[g] + GRP], ps[:, g % 2, :], ACT.Silu).then_inc(m_silu, 1)
                    if g:
                        hidden_hi(i, g - 1)
                    elif not first:
                        hidden_hi(i - 1, NG - 1)
                    if g == 3:
                        act.wait_ge(m_gt, i + 1)
                        act.activation(r4[:, 512:512 + SEQ], ps[:, 7, 0:SEQ], ACT.Copy).then_inc(m_gtc, 1)
                    if ahead and g >= NG - 2:
                        gather_hi(i + 1, 1 - par, g - (NG - 2))
                upto_c(PER_ITEM - 1)

            def drain(i):
                hidden_hi(i, NG - 1)
                copy_y(i, PER_ITEM - 1)

            item(0, 0, True, True)
            with act.Fori(0, EXPERTS // 2 - 1) as j:
                item(j * 2 + 1, 1, False, True)
                item(j * 2 + 2, 0, False, True)
            item(EXPERTS - 1, 1, False, False)
            drain(EXPERTS - 1)
            act.wait_ge(route_ready, 1)
            spare = act.value_load(info[0:1, ITEMS:ITEMS + 1], min_val=0, max_val=SPARE)
            with act.Fori(EXPERTS, ITEMS) as i:
                with act.If(i < spare + EXPERTS):
                    item(i, 0, True, False)
                    drain(i)
            root(T)

        @block.vector
        def _(dve):
            steps = [0]

            def link(ins):
                steps[0] += 1
                ins.then_inc(v_step, 1)
                dve.wait_ge(v_step, steps[0])

            done, sums, gates = [0], [0], [0]

            def ada_quarter(a, q):
                l, v = ADA[a]
                r = RAW_OF["ada", a, q]
                dve.wait_ge(raw_full[r % NRAW], 16 * (r // NRAW + 1))
                if q == 0 and a:
                    dve.wait_ge(ada_full, sum(2 if ADA[b][1] in (G_M, G_F) else 1 for b in range(a)))
                for kk in range(2):
                    w = raw[:, r % NRAW, kk * D:(kk + 1) * D]
                    c = cact[:, 2 * q + kk:2 * q + kk + 1]
                    if q == 0 and kk == 0:
                        link(dve.tensor_scalar(acc[:, :], w, c, None, ALU.mult))
                    else:
                        m = dve.scalar_tensor_tensor(acc[:, :], w, c, acc[:, :], ALU.mult, ALU.add)
                        if kk == 0:
                            link(m)
                m.then_inc(raw_done, 1)
                dve.wait_ge(raw_done, r + 1)
                if q == 3 and v in (G_M, G_F):
                    for k in range(K):
                        m = dve.scalar_tensor_tensor(acc[:, k * P:(k + 1) * P], ident[:, :], col(COL_ADA + (l * 6 + v) * K + k),
                                                     acc[:, k * P:(k + 1) * P], ALU.mult, ALU.add)
                    m.then_inc(ada_acc, 1)
                    gates[0] += 1
                    dve.wait_ge(ada_acc, gates[0])

            def ada_use(a, half):
                l, v = ADA[a]
                sums[0] += 1
                dve.wait_ge(ada_full, sums[0])
                n = 2 * l + (v >= SH_F)
                if v in (G_M, G_F):
                    gate, arrived = (gate_m, post_m_in) if v == G_M else (gate_f, post_f_in)
                    dve.wait_ge(arrived, 16 * (l + 1))
                    g = gate[:, half * 512:(half + 1) * 512]
                    dve.tensor_tensor(g, ps[:, 7, :], g, ALU.mult).then_inc(ada_used, 1)
                    dve.wait_ge(ada_used, sums[0])
                    return
                bias = cols[:, COL_ADA + (l * 6 + v) * K:COL_ADA + (l * 6 + v + 1) * K]
                what = AB[:, n, 0 if v in (SC_M, SC_F) else 1, :]
                dve.tensor_tensor(what, ps[:, 7, 0:K], bias, ALU.add).then_inc(ada_used, 1)
                dve.wait_ge(ada_used, sums[0])
                if v in (SC_M, SC_F):
                    link(dve.scalar_tensor_tensor(what, what, 1.0, cols[:, COL_NORM + n * K:COL_NORM + (n + 1) * K], ALU.add, ALU.mult))

            def lo_part(s):
                r, e = RAW_OF["w", s, 0], WEIGHTS[s][3]
                dve.wait_ge(hi_done, s + 1)
                dve.tensor_tensor(lo[:, s % NSPLIT, 0:e], raw[:, r % NRAW, 0:e], hi[:, s % NSPLIT, 0:e].bitcast(f32),
                                  ALU.subtract).then_inc(raw_done, 1)

            def upto(name, ahead=2):
                while done[0] < min(CHUNK[name] + ahead + 1, NW):
                    s = done[0]
                    for a, (_, _, at) in enumerate(ADA_AT, len(ADA_FIRST)):
                        if at <= s < at + 4:
                            ada_quarter(a, s - at)
                    lo_part(s)
                    for a, half, _, use in SUMS:
                        if use == s:
                            ada_use(a, half)
                    done[0] += 1

            roots = [0]

            def root(n):
                link(dve.tensor_scalar(ms[:, 0:n], ms[:, 0:n], EPS, None, ALU.add))
                dve.reciprocal(ms[:, 0:n], ms[:, 0:n]).then_inc(var_ready, 1)
                roots[0] += 1
                dve.wait_ge(rstd_ready, roots[0])

            def mean_square(src, scratch, at, width):
                return dve.scalar_tensor_tensor(scratch, src, 1.0 / width, src, ALU.mult, ALU.mult, accum_out=ms[:, at:at + 1])

            def h_part(n, first):
                for t in range(T):
                    m = mean_square(x[:, t, :], xn[:, t, :], t, D)
                link(m)
                root(T)
                for t in range(T):
                    dve.tensor_scalar(xn[:, t, :], x[:, t, :], rstd[:, t:t + 1], None, ALU.mult).then_inc(xn_ready, 1)
                if first:
                    upto(first, 1)

                def full(b):
                    dve.wait_ge(xt_full, 4 * n + b + 1)
                    for k in (2 * b, 2 * b + 1):
                        m = dve.tensor_scalar(hf[:, k, :], ps[:, b, (k % 2) * SEQ:(k % 2 + 1) * SEQ],
                                              AB[:, n, 0, k:k + 1], AB[:, n, 1, k:k + 1], ALU.mult, ALU.add)
                    m.then_inc(hf_ready, 1)

                def rest(b):
                    dve.wait_ge(hth_ready, 4 * n + b + 1)
                    dve.tensor_tensor(hTl[:, 2 * b:2 * b + 2, :], hf[:, 2 * b:2 * b + 2, :],
                                      hTh[:, 2 * b:2 * b + 2, :].bitcast(f32), ALU.subtract).then_inc(ht_ready, 1)

                full(0)
                for b in range(1, 4):
                    full(b)
                    rest(b - 1)
                rest(3)

            def post(n, y, gate):
                for t in range(T):
                    m = mean_square(y[:, t, :], r3[:, t * D:(t + 1) * D], t, D)
                link(m)
                root(T)
                for t in range(T):
                    m = dve.scalar_tensor_tensor(y[:, t, :], y[:, t, :], rstd[:, t:t + 1], gate[:, :], ALU.mult, ALU.mult)
                    if t == T - 1:
                        link(m)
                for t in range(T):
                    dve.tensor_tensor(x[:, t, :], x[:, t, :], y[:, t, :], ALU.add).then_inc(x_done, 1)
                    dve.wait_ge(x_done, T * n + t + 1)

            TWO_PI = 2.0 * np.pi
            C1 = 6.28125
            C2 = float(np.round((TWO_PI - C1) * 2 ** 20) / 2 ** 20)
            C3 = float(TWO_PI - C1 - C2)
            BIG = 1.5 * 2.0 ** 23
            LIMIT = float(np.nextafter(np.float32(np.pi), np.float32(0)))
            dve.wait_ge(consts_in, 16)
            dve.wait_ge(small_in, 32)
            dve.wait_ge(pool_setup, 6)
            link(dve.tensor_copy(posf[:, :], pos_i[:, :]))
            for t in range(T):
                m = dve.tensor_scalar(ang[:, t, :], inv[:, :], posf[:, t:t + 1], None, ALU.mult)
            link(m)
            for dst, quarter in ((cosT, 0.25), (sinT, 0.0)):
                r = rope_t[:, 0, 0:T * HALF].rearrange("p (t d) -> p t d", t=T)
                link(dve.tensor_scalar(dst[:, :, :], ang[:, :, :], 1.0 / TWO_PI, quarter, ALU.mult, ALU.add))
                link(dve.tensor_scalar(dst[:, :, :], dst[:, :, :], BIG, None, ALU.add))
                link(dve.tensor_scalar(dst[:, :, :], dst[:, :, :], -BIG, None, ALU.add))
                link(dve.scalar_tensor_tensor(r, dst[:, :, :], -C1, ang[:, :, :], ALU.mult, ALU.add))
                link(dve.scalar_tensor_tensor(r, dst[:, :, :], -C2, r, ALU.mult, ALU.add))
                link(dve.scalar_tensor_tensor(r, dst[:, :, :], -C3, r, ALU.mult, ALU.add))
                link(dve.tensor_scalar(r, r, quarter * TWO_PI, LIMIT, ALU.add, ALU.min))
                m = dve.tensor_scalar(dst[:, :, :], r, -LIMIT, None, ALU.max)
                if dst is cosT:
                    link(m)
            m.then_inc(ang_ready, 1)

            dve.wait_ge(cact_ready, 1)
            for a in range(len(ADA_FIRST)):
                for q in range(4):
                    ada_quarter(a, q)
                ada_use(a, 0)
            dve.wait_ge(x_in, 16)

            def mixer(l):
                h_part(2 * l, f"m{l}.cq0")
                upto(f"m{l}.kr1")
                dve.wait_ge(lat_copied, 4 * l + 4)
                for t in range(T):
                    mean_square(lat[:, t, 0:QR], r6[:, t * QR:(t + 1) * QR], t, QR)
                for t in range(T):
                    m = mean_square(lat[:, t, QR:], r6[:, T * QR + t * KVR:T * QR + (t + 1) * KVR], T + t, KVR)
                link(m)
                root(2 * T)
                for t in range(T):
                    dve.tensor_scalar(lat[:, t, 0:QR], lat[:, t, 0:QR], rstd[:, t:t + 1], None, ALU.mult)
                    m = dve.tensor_scalar(lat[:, t, QR:], lat[:, t, QR:], rstd[:, T + t:T + t + 1], None, ALU.mult)
                m.then_inc(lat_ready, 1)
                upto(f"m{l}.v1")
                for kk in range(LATC):
                    dve.wait_ge(latTh_ready, LATC * l + min(kk - kk % 2 + 2, LATC))
                    at = COL_QN + l * QC + kk if kk < QC else COL_KVN + l * KC + kk - QC
                    dve.scalar_tensor_tensor(bTl[:, kk, :], ps[:, [5, 6, 0][kk // 2], (kk % 2) * SEQ:(kk % 2 + 1) * SEQ],
                                             col(at), bTh[:, kk, :].bitcast(f32), ALU.mult, ALU.subtract).then_inc(latT_ready, 1)
                dve.wait_ge(vu_done, 4 * l + 2)
                for t in range(T):
                    m = dve.bn_stats(bn[:, t, :], v_g[:, t, :])
                link(m)
                for t in range(T):
                    m = dve.bn_aggr(mv[:, t, :], bn[:, t, :])
                link(m)
                link(dve.tensor_copy(ms[:, 0:T], mv[:, :, 1]))
                root(T)
                for t in range(T):
                    m = dve.tensor_scalar(v_g[:, t, :], v_g[:, t, :], mv[:, t, 0:1], rstd[:, t:t + 1], ALU.subtract, ALU.mult)
                link(m)
                dve.wait_ge(ln_in, 32 * (l + 1))
                for t in range(T):
                    m = dve.tensor_tensor(v_g[:, t, :], v_g[:, t, :], ln_g, ALU.mult)
                link(m)
                for t in range(T):
                    m = dve.tensor_tensor(v_g[:, t, :], v_g[:, t, :], ln_b, ALU.add)
                m.then_inc(vn_ready, 1)
                dve.wait_ge(vn_ready, l + 1)
                upto(f"m{l}.ukv")
                dve.wait_ge(rope_ready, 1)
                dve.wait_ge(attn_copied, 8 * l + 4)
                shape = [P, T, HEADS + 1, HALF]
                x1, x2 = qk[:, :, :, NOPE:NOPE + HALF], qk[:, :, :, NOPE + HALF:QKD]
                cb, sbc = (z[:, :, :].unsqueeze(2).to_broadcast(shape) for z in (cosT, sinT))
                t0, t1 = (rope_t[:, i, :].rearrange("p (t h d) -> p t h d", t=T, h=HEADS + 1) for i in range(2))
                dve.tensor_tensor(t0, x1, sbc, ALU.mult)
                link(dve.tensor_tensor(t1, x2, sbc, ALU.mult))
                dve.tensor_tensor(x1, x1, cb, ALU.mult)
                link(dve.tensor_tensor(x2, x2, cb, ALU.mult))
                dve.tensor_tensor(x1, x1, t1, ALU.subtract)
                link(dve.tensor_tensor(x2, x2, t0, ALU.add))
                for t in range(T):
                    m = dve.tensor_copy(k_tok[:, t, :, NOPE:QKD],
                                        qk[:, t, HEADS, NOPE:QKD].unsqueeze(1).to_broadcast([P, HEADS, ROPE]))
                m.then_inc(qk_ready, 1)
                for j in range(4):
                    dve.wait_ge(kT_full, 4 * l + j + 1)
                    dve.tensor_copy(kT[:, 2 * j:2 * j + 2, :], ps[0:QKD, 3 + j, :].rearrange("p (h s) -> p h s", h=2)).then_inc(kT_copied, 1)
                dve.wait_ge(vu_done, 4 * l + 4)
                for t in range(T):
                    dve.wait_ge(z_full, T * l + t + 1)
                    for g in range(GROUPS):
                        u = u_g[:, t, g * GDIM:(g + 1) * GDIM]
                        m = dve.scalar_tensor_tensor(u, ps[:, t, g * GDIM:(g + 1) * GDIM], col(COL_BS + l * GROUPS + g), u, ALU.add, ALU.mult)
                    m.then_inc(uz_ready, 1)
                for u in range(6):
                    heads, keys = (4, P) if u < 2 else (2, SEQ)
                    dve.wait_ge(sc_full, 6 * l + u + 1)
                    if u >= 4:
                        dve.wait_ge(pT_full, 6 * l + u - 3)
                    sv = S[:, u % 4, :].rearrange("p (h s) -> p h s", h=heads)
                    mb = mask[:, 2 * P - keys:2 * P].unsqueeze(1).to_broadcast([P, heads, keys])
                    dve.tensor_tensor(sv, ps[:, [2, 3, 4, 5, 6, 0][u], :].rearrange("p (h s) -> p h s", h=heads), mb, ALU.add).then_inc(s_ready, 1)
                    dve.wait_ge(s_ready, 6 * l + u + 1)
                    link(dve.reduce_max(mx[:, u, 0:heads], sv, AX))
                    dve.tensor_scalar(nmx[:, u, 0:heads], mx[:, u, 0:heads], -(QKD ** -0.5), None, ALU.mult).then_inc(nmx_ready, 1)
                for t in range(T):
                    dve.wait_ge(p_ready, 6 * l + (2, 6)[t])
                    if t == 0:
                        src, dst = psum_p[:, 0:2, 0:4], rinv[:, 0, :].rearrange("p (a b) -> p a b", a=2)
                    else:
                        src, dst = psum_p[:, 2:6, 0:2], rinv[:, 1, :].rearrange("p (a b) -> p a b", a=4)
                    link(dve.reciprocal(dst, src))
                    dve.wait_ge(o_full, T * l + t + 1)
                    dve.tensor_tensor(o_tok[:, t, :].rearrange("p (h d) -> p h d", h=HEADS), ps[:, 2 + t, :].rearrange("p (h d) -> p h d", h=HEADS),
                                      rinv[:, t, :].unsqueeze(2).to_broadcast([P, HEADS, VD]), ALU.mult).then_inc(o_ready, 1)
                for i in range(2 * T):
                    t = i % T
                    dve.wait_ge(brTh_ready, 4 * l + i + 1)
                    dst = slice(4 * (i // T), 4 * (i // T) + 4), slice(t * P, (t + 1) * P)
                    dve.tensor_tensor(bTl[:, dst[0], dst[1]], ps[:, [4, 5, 6, 0][i], :].rearrange("p (c s) -> p c s", c=4),
                                      bTh[:, dst[0], dst[1]].bitcast(f32), ALU.subtract).then_inc(brT_ready, 1)
                for j in range(4):
                    upto(f"m{l}.ab{j}")
                    dve.wait_ge(used, CHUNK[f"m{l}.ab{j}"] + 1)
                    for m_ in range(2):
                        mm = 2 * j + m_
                        sg = S[:, mm % 4, :]
                        dve.wait_ge(sig_done, 8 * l + mm + 1)
                        link(dve.tensor_tensor(sg, sg, ps[:, [3, 5][j % 2] + m_, :], ALU.mult))
                        dve.tensor_tensor(merged[:, mm, :], sg[:, 0:SEQ], sg[:, SEQ:2 * SEQ], ALU.add).then_inc(mg_done, 1)
                for h in range(2):
                    dve.wait_ge(mth_ready, 2 * l + h + 1)
                    dve.tensor_tensor(hTl[:, 4 * h:4 * h + 4, :], merged[:, 4 * h:4 * h + 4, :],
                                      hTh[:, 4 * h:4 * h + 4, :].bitcast(f32), ALU.subtract).then_inc(mt_ready, 1)
                upto(f"m{l}.wo3")
                dve.wait_ge(y_copied, T * 2 * l + T)
                post(2 * l, y_sb, gate_m)

            def ffn():
                h_part(1, "fg0")
                for j in range(FG):
                    upto(f"fu{j}")
                    for i in (2 * j, 2 * j + 1):
                        a = r4[:, (i % 4) * SEQ:(i % 4 + 1) * SEQ]
                        dve.wait_ge(silu_done, i + 1)
                        dve.tensor_tensor(a, a, ps[:, i % 3, SEQ:2 * SEQ], ALU.mult).then_inc(hb_done, 1)
                    for i in (2 * j, 2 * j + 1):
                        dve.wait_ge(hbh_ready, i + 1)
                        dve.tensor_tensor(bTl[:, i % K, :], r4[:, (i % 4) * SEQ:(i % 4 + 1) * SEQ], bTh[:, i % K, :].bitcast(f32),
                                          ALU.subtract).then_inc(hb_ready, 1)
                upto(f"fd{FG - 1}")
                dve.wait_ge(y_copied, 2 * T)
                post(1, y_sb, gate_f)

            mixer(0)
            ffn()
            mixer(1)
            h_part(3, None)

            def route():
                E = EXPERTS
                at = [0]

                def tile(*shape):
                    n = int(np.prod(shape))
                    v = r4[:, at[0]:at[0] + n]
                    at[0] += n
                    return v.rearrange("p (a b) -> p a b", a=shape[0]) if len(shape) == 2 else (
                        v.rearrange("p (a b c) -> p a b c", a=shape[0], b=shape[1]) if len(shape) == 3 else v)

                lg, rank, sel = tile(T, E), tile(T, E), tile(T, E)
                cmp, eq = tile(T, E, E), tile(T, E, E)
                at[0] = 512
                ex = tile(T, E)
                ov, orank, one = tile(E), tile(E), tile(E)
                ee, w2 = tile(E, E), tile(T, E)
                dve.wait_ge(router_full, 1)
                link(dve.tensor_tensor(lg, ps[:, 7, 0:T * E].rearrange("p (t e) -> p t e", t=T),
                                       rb[:, :].unsqueeze(1).to_broadcast([P, T, E]), ALU.add))
                for t in range(T):
                    other = lg[:, t, :].unsqueeze(1).to_broadcast([P, E, E])
                    own = lg[:, t, :].unsqueeze(2).to_broadcast([P, E, E])
                    dve.tensor_tensor(cmp[:, t], other, own, ALU.is_gt)
                    link(dve.tensor_tensor(eq[:, t], other, own, ALU.is_equal))
                    link(dve.tensor_tensor(eq[:, t], eq[:, t], lt_mask[:, :, :], ALU.mult))
                    link(dve.tensor_tensor(cmp[:, t], cmp[:, t], eq[:, t], ALU.add))
                    link(dve.reduce_sum(rank[:, t, :], cmp[:, t], AX))
                dve.tensor_scalar(sel, rank, 1.5, None, ALU.is_lt).then_inc(sel_ready, 1)
                link(dve.reduce_max(small[:, 0:T], lg, AX))
                for t in range(T):
                    m = dve.tensor_scalar(ex[:, t, :], lg[:, t, :], small[:, t:t + 1], None, ALU.subtract)
                m.then_inc(ex_in, 1)
                dve.wait_ge(ex_done, 1)
                dve.wait_ge(sel_ready, 1)
                link(dve.tensor_tensor(ex, ex, sel, ALU.mult))
                link(dve.reduce_sum(small[:, T:2 * T], ex, AX))
                link(dve.reciprocal(small[:, T:2 * T], small[:, T:2 * T]))
                for t in range(T):
                    link(dve.tensor_scalar(gate_tab[:, t, 0:E], ex[:, t, :], small[:, T + t:T + t + 1], None, ALU.mult))
                dve.wait_ge(count_full, 1)
                for t in range(T):
                    slot = pos_tab[:, t, 0:E]
                    link(dve.scalar_tensor_tensor(slot, ps[:, 7, 32 + t * E:32 + (t + 1) * E], 1.0, sel[:, t, :], ALU.add, ALU.mult))
                    link(dve.tensor_scalar(slot, slot, -1.0, None, ALU.add))
                link(dve.tensor_scalar(ov, ps[:, 7, 32 + T * E:32 + (T + 1) * E], P + 0.5, None, ALU.is_gt))
                link(dve.memset(info_f[:, :], 0.0))
                dve.reduce_sum(info_f[:, ITEMS:ITEMS + 1], ov, AX)
                link(dve.tensor_tensor(ee, lt_mask[:, :, :], ov.unsqueeze(1).to_broadcast([P, E, E]), ALU.mult))
                link(dve.reduce_sum(orank, ee, AX))
                for j in range(SPARE):
                    link(dve.tensor_scalar(one, orank, float(j), None, ALU.is_equal))
                    link(dve.tensor_tensor(one, one, ov, ALU.mult))
                    link(dve.tensor_tensor(w2[:, 0, :], one, eidx[:, :], ALU.mult))
                    link(dve.reduce_sum(info_f[:, E + j:E + j + 1], w2[:, 0, :], AX))
                    for t in range(T):
                        link(dve.scalar_tensor_tensor(w2[:, t, :], pos_tab[:, t, 0:E], 1.0 - P, one, ALU.add, ALU.mult))
                    link(dve.reduce_sum(pos_tab[:, :, E + j:E + j + 1].rearrange("p t o -> p (t o)"), w2, AX))
                    link(dve.tensor_scalar(pos_tab[:, :, E + j], pos_tab[:, :, E + j], -1.0, None, ALU.add))
                    for t in range(T):
                        link(dve.tensor_tensor(w2[:, t, :], gate_tab[:, t, 0:E], one, ALU.mult))
                    link(dve.reduce_sum(gate_tab[:, :, E + j:E + j + 1].rearrange("p t o -> p (t o)"), w2, AX))
                dve.tensor_copy(info[:, :], info_f[:, :]).then_inc(route_ready, 1)

            route()
            dve.wait_ge(route_ready, 1)
            dve.memset(r6[:, 0:T * D], 0.0).then_inc(m_acc, 1)

            def item_lo(i, lo_c, hi_c):
                for c in range(lo_c, hi_c):
                    slot, s = (NR + c) % NRAW, (NW + c) % NSPLIT
                    dve.wait_ge(hi_done, i * PER_ITEM + (NW + c + 1))
                    dve.tensor_tensor(lo[:, s, :], raw[:, slot, :], hi[:, s, :].bitcast(f32), ALU.subtract).then_inc(raw_done, 1)

            def select(i):
                dve.tensor_copy(pg[:, 0, :], pos_tab[:, :, bass.ds(i, 1)].rearrange("p t o -> p (t o)"))
                dve.tensor_copy(pg[:, 1, :], gate_tab[:, :, bass.ds(i, 1)].rearrange("p t o -> p (t o)")).then_inc(v_loop, 1)
                dve.wait_ge(v_loop, i + 1)
                for t in range(T):
                    dve.tensor_scalar(r4[:, t * P:(t + 1) * P], slots[:, :], pg[:, 0, t:t + 1], None, ALU.is_equal)
                    m = dve.tensor_scalar(r4[:, 256 + t * P:256 + (t + 1) * P], slots[:, :], pg[:, 0, t:t + 1], pg[:, 1, t:t + 1],
                                          ALU.is_equal, ALU.mult)
                m.then_inc(m_pos, 1)

            def gathered(i, h):
                dve.wait_ge(m_gath, i * 2 + h + 1)
                for kk in range(4):
                    k = 4 * h + kk
                    m = dve.tensor_scalar(r3[:, k * P:(k + 1) * P], ps[:, 7, kk * P:(kk + 1) * P],
                                          AB[:, 3, 0, k:k + 1], AB[:, 3, 1, k:k + 1], ALU.mult, ALU.add)
                m.then_inc(m_xf, 1)

            def gathered_lo(i, par, h):
                dve.wait_ge(m_xh, i * 2 + h + 1)
                at = slice(par * P, (par + 1) * P)
                dve.tensor_tensor(hTl[:, 4 * h:4 * h + 4, at], r3[:, 512 * h:512 * h + 512].rearrange("p (k s) -> p k s", k=4),
                                  hTh[:, 4 * h:4 * h + 4, at].bitcast(f32), ALU.subtract).then_inc(m_x, 1)

            def hidden(i, g, first):
                a = r3[:, HS[g]:HS[g] + GRP]
                dve.wait_ge(m_silu, i * NG + g + 1)
                dve.wait_ge(used, i * PER_ITEM + (NW + spot("w3", g, 1, first) + 1))
                dve.tensor_tensor(a, a, ps[:, 2 + g % 2, :], ALU.mult).then_inc(m_hb, 1)

            def hidden_lo(i, g):
                dve.wait_ge(m_hh, i * NG + g + 1)
                dve.tensor_tensor(bTl[:, 0:4, 0:P], ps[:, 6, :].rearrange("p (c s) -> p c s", c=4),
                                  bTh[:, 0:4, 0:P].bitcast(f32), ALU.subtract).then_inc(m_h, 1)

            def add_y(i, q):
                ya = y_exp[:, q // 2, (q % 2) * 512:(q % 2 + 1) * 512]
                if q == 0:
                    dve.wait_ge(m_acc, i * 4 + 1)
                dve.wait_ge(m_sc, i * 4 + q + 1)
                dve.tensor_tensor(ya, ya, ps[:, 7, :], ALU.add).then_inc(m_acc, 1)

            def item(i, par, first, ahead):
                if first:
                    if not ahead:
                        dve.wait_ge(m_gt, i)
                    select(i)
                    for h in range(2):
                        gathered(i, h)
                    for h in range(2):
                        gathered_lo(i, par, h)
                    item_lo(i, 0, 2)
                at = [2 if first else 0]

                def upto_c(c):
                    item_lo(i, at[0], c + 1)
                    at[0] = max(at[0], c + 1)

                for g in range(NG):
                    upto_c(spot("w1", g, 1, first) + 2)
                    if g:
                        hidden_lo(i, g - 1)
                    elif not first:
                        hidden_lo(i - 1, NG - 1)
                    if not first and g in (1, 2):
                        add_y(i - 1, 2 * g - 2)
                    if ahead and g == 4:
                        dve.wait_ge(m_gt, i + 1)
                        select(i + 1)
                    if ahead and g >= NG - 2:
                        gathered(i + 1, g - (NG - 2))
                    upto_c(spot("w3", g, 1, first) + 2)
                    hidden(i, g, first)
                    if not first and g in (1, 2):
                        add_y(i - 1, 2 * g - 1)
                    if ahead and g >= NG - 2:
                        gathered_lo(i + 1, 1 - par, g - (NG - 2))
                upto_c(PER_ITEM - 1)

            def drain(i):
                hidden_lo(i, NG - 1)
                for q in range(4):
                    add_y(i, q)
                dve.wait_ge(m_acc, i * 4 + 5)
                dve.memset(small[:, 0:1], 0.0)

            item(0, 0, True, True)
            with dve.Fori(0, EXPERTS // 2 - 1) as j:
                item(j * 2 + 1, 1, False, True)
                item(j * 2 + 2, 0, False, True)
            item(EXPERTS - 1, 1, False, False)
            drain(EXPERTS - 1)
            spare = dve.value_load(info[0:1, ITEMS:ITEMS + 1], min_val=0, max_val=SPARE)
            with dve.Fori(EXPERTS, ITEMS) as i:
                with dve.If(i < spare + EXPERTS):
                    item(i, 0, True, False)
                    drain(i)
            post(3, y_exp, gate_f)

        @block.tensor
        def _(pe):
            summed, gates = [0], [0]

            def three(o, wh, wl, mh, ml, first, last):
                pe.matmul(o, wh, mh, start=first, stop=False)
                pe.matmul(o, wh, ml, start=False, stop=False)
                return pe.matmul(o, wl, mh, start=False, stop=last)

            def ada_sum(a, half):
                l, v = ADA[a]
                if v in (G_M, G_F):
                    if half == 0:
                        gates[0] += 1
                    pe.wait_ge(ada_acc, gates[0])
                else:
                    pe.wait_ge(raw_done, RAW_OF["ada", a, 3] + 1)
                if summed[0]:
                    pe.wait_ge(ada_used, summed[0])
                if v in (G_M, G_F):
                    m = pe.matmul(ps[:, 7, :], ones[:, :], acc[:, half * 512:(half + 1) * 512], start=True, stop=True)
                else:
                    for k in range(K):
                        m = pe.matmul(ps[:, 7, k:k + 1], acc[:, k * P:(k + 1) * P], ones[:, 0:1], start=True, stop=True)
                m.then_inc(ada_full, 1)
                summed[0] += 1

            def chunk(name):
                s = CHUNK[name]
                pe.wait_ge(raw_done, RAW_OF["w", s, 0] + 1)
                return hi[:, s % NSPLIT, :], lo[:, s % NSPLIT, :]

            def finish(name, m):
                m.then_inc(used, 1)
                for a, half, after, _ in SUMS:
                    if after == CHUNK[name]:
                        ada_sum(a, half)

            def h_turn(n):
                pe.wait_ge(xn_ready, T * (n + 1))
                for b in range(4):
                    for kk in range(2):
                        for t in range(T):
                            m = pe.transpose(ps[:, b, kk * SEQ + t * P:kk * SEQ + (t + 1) * P],
                                             xn[:, t, (2 * b + kk) * P:(2 * b + kk + 1) * P], ident[:, :])
                    m.then_inc(xt_full, 1)

            def by_token(name, l, width, banks):
                for h in range(2):
                    wh, wl = chunk(f"m{l}.{name}{h}")
                    for t in range(T):
                        for kk in range(4):
                            k = 4 * h + kk
                            w = slice(kk * width, (kk + 1) * width)
                            m = three(ps[:, banks[t], 0:width], hTh[:, k, t * P:(t + 1) * P], hTl[:, k, t * P:(t + 1) * P],
                                      wh[:, w], wl[:, w], k == 0, k == K - 1)
                    finish(f"m{l}.{name}{h}", m)

            pe.wait_ge(pool_setup, 6)
            for a in range(len(ADA_FIRST)):
                ada_sum(a, 0)

            def mixer(l):
                h_turn(2 * l)
                pe.wait_ge(ht_ready, 8 * l + 4)
                by_token("cq", l, QR, (4, 5))
                by_token("kr", l, KVR + ROPE, (6, 0))
                by_token("v", l, GW, (1, 2))
                pe.wait_ge(lat_ready, l + 1)
                for kk in range(LATC):
                    for t in range(T):
                        m = pe.transpose(ps[:, [5, 6, 0][kk // 2], (kk % 2) * SEQ + t * P:(kk % 2) * SEQ + (t + 1) * P],
                                         lat[:, t, kk * P:(kk + 1) * P], ident[:, :])
                    if kk % 2 or kk == LATC - 1:
                        m.then_inc(latT_full, 1)
                by_token("u", l, GW, (3, 4))
                pe.wait_ge(latT_ready, LATC * (l + 1))
                for h in range(2):
                    wh, wl = chunk(f"m{l}.uq{h}")
                    for t in range(T):
                        if (h, t) == (1, 1):
                            pe.wait_ge(vu_done, 4 * l + 1)
                        for kk in range(QC):
                            w = slice(kk * QR, (kk + 1) * QR)
                            m = three(ps[:, [5, 6, 0, 1][2 * h + t], 0:QR], bTh[:, kk, t * P:(t + 1) * P], bTl[:, kk, t * P:(t + 1) * P],
                                      wh[:, w], wl[:, w], kk == 0, kk == QC - 1)
                    finish(f"m{l}.uq{h}", m)
                wh, wl = chunk(f"m{l}.ukv")
                for half in range(2):
                    for t in range(T):
                        i = 2 * half + t
                        if i < 3:
                            pe.wait_ge(vu_done, 4 * l + 2 + i)
                        else:
                            pe.wait_ge(attn_copied, 8 * l + 1)
                        for kk in range(KC):
                            w = slice(kk * D + half * 512, kk * D + (half + 1) * 512)
                            m = three(ps[:, 2 + i, :], bTh[:, QC + kk, t * P:(t + 1) * P], bTl[:, QC + kk, t * P:(t + 1) * P],
                                      wh[:, w], wl[:, w], kk == 0, kk == KC - 1)
                finish(f"m{l}.ukv", m)
                pe.wait_ge(attn_copied, 8 * l + 8)
                pe.wait_ge(qk_ready, l + 1)
                for j in range(4):
                    for hh in range(2):
                        for t in range(T):
                            m = pe.transpose(ps[0:QKD, [6, 0, 1, 2][j], hh * SEQ + t * P:hh * SEQ + (t + 1) * P],
                                             qk[:, t, 2 * j + hh, :], ident[:, :])
                    m.then_inc(qT_full, 1)
                for j in range(4):
                    if j == 3:
                        pe.wait_ge(qT_copied, 4 * l + 1)
                    for hh in range(2):
                        for t in range(T):
                            m = pe.transpose(ps[0:QKD, 3 + j, hh * SEQ + t * P:hh * SEQ + (t + 1) * P],
                                             k_tok[:, t, 2 * j + hh, :], ident[:, :])
                    m.then_inc(kT_full, 1)
                pe.wait_ge(vn_ready, l + 1)
                pe.wait_ge(ws_masked, l + 1)
                for t in range(T):
                    pe.wait_ge(qT_copied, 4 * l + 2 + t)
                    for g in range(GROUPS):
                        m = pe.matmul(ps[:, t, g * GDIM:(g + 1) * GDIM], ws[:, g, :], v_g[:, t, g * GDIM:(g + 1) * GDIM],
                                      start=True, stop=True)
                    m.then_inc(z_full, 1)
                pe.wait_ge(qT_copied, 4 * l + 4)
                pe.wait_ge(kT_copied, 4 * l + 4)
                for u in range(6):
                    t, heads = (0, range(4 * u, 4 * u + 4)) if u < 2 else (1, (2 * u - 4, 2 * u - 3))
                    keys = (t + 1) * P
                    if u == 5:
                        pe.wait_ge(uz_ready, T * l + 1)
                    for n, h in enumerate(heads):
                        m = pe.matmul(ps[:, [2, 3, 4, 5, 6, 0][u], n * keys:(n + 1) * keys], qT[:, h, t * P:(t + 1) * P],
                                      kT[:, h, 0:keys], start=True, stop=True)
                    m.then_inc(sc_full, 1)

                def turn_p(u):
                    if u == 0:
                        pe.wait_ge(uz_ready, T * l + 2)
                    pe.wait_ge(p_ready, 6 * l + u + 1)
                    for c in range(4):
                        m = pe.transpose(ps[:, 1 + u, c * P:(c + 1) * P], S[:, u % 4, c * P:(c + 1) * P], ident[:, :])
                    m.then_inc(pT_full, 1)

                def weigh_v(t):
                    pe.wait_ge(pT_copied, 6 * l + (2, 6)[t])
                    for h in range(HEADS):
                        for kb in range(t + 1):
                            slot, c = (h // 4, h % 4) if t == 0 else ((2 + h // 2) % 4, (h % 2) * 2 + kb)
                            m = pe.matmul(ps[:, 2 + t, h * VD:(h + 1) * VD], pT[:, slot, c * P:(c + 1) * P],
                                          v_tok[:, kb, h * VD:(h + 1) * VD], start=(kb == 0), stop=(kb == t))
                    m.then_inc(o_full, 1)

                for u in range(4):
                    turn_p(u)
                weigh_v(0)
                turn_p(4)
                turn_p(5)
                weigh_v(1)
                for i, src in enumerate((u_g, u_g, o_tok, o_tok)):
                    t = i % T
                    if i >= T:
                        pe.wait_ge(o_ready, T * l + t + 1)
                    for c in range(4):
                        m = pe.transpose(ps[:, [4, 5, 6, 0][i], c * P:(c + 1) * P], src[:, t, c * P:(c + 1) * P], ident[:, :])
                    m.then_inc(brT_full, 1)
                for j in range(4):
                    for half, name in enumerate((f"m{l}.ga{j}", f"m{l}.gb{j}")):
                        wh, wl = chunk(name)
                        for m_ in range(2):
                            if j and half == 0:
                                pe.wait_ge(sig_done, 8 * l + 2 * (j - 1) + m_ + 1)
                            for k in range(K):
                                w = slice(k * 2 * P + m_ * P, k * 2 * P + (m_ + 1) * P)
                                m = three(ps[:, 1 + m_, half * SEQ:(half + 1) * SEQ], wh[:, w], wl[:, w], hTh[:, k, :], hTl[:, k, :],
                                          k == 0, k == K - 1)
                        finish(name, m)
                    wh, wl = chunk(f"m{l}.ab{j}")
                    if j == 0:
                        pe.wait_ge(brT_ready, 4 * l + 4)
                    for m_ in range(2):
                        if j >= 2:
                            pe.wait_ge(mg_done, 8 * l + 2 * (j - 2) + m_ + 1)
                        for k in range(K):
                            w = slice(k * 2 * P + m_ * P, k * 2 * P + (m_ + 1) * P)
                            m = three(ps[:, [3, 5][j % 2] + m_, (k // 4) * SEQ:(k // 4 + 1) * SEQ], wh[:, w], wl[:, w], bTh[:, k, :], bTl[:, k, :],
                                      k % 4 == 0, k % 4 == 3)
                    finish(f"m{l}.ab{j}", m)
                for j in range(4):
                    wh, wl = chunk(f"m{l}.wo{j}")
                    pe.wait_ge(mt_ready, 2 * l + 1 + j // 2)
                    for t in range(T):
                        for half in range(2):
                            for kk in range(2):
                                k = 2 * j + kk
                                w = slice(kk * D + half * 512, kk * D + (half + 1) * 512)
                                m = three(ps[:, 2 * t + half, :], hTh[:, k, t * P:(t + 1) * P], hTl[:, k, t * P:(t + 1) * P],
                                          wh[:, w], wl[:, w], k == 0, k == K - 1)
                    finish(f"m{l}.wo{j}", m)

            def ffn():
                h_turn(1)
                pe.wait_ge(ht_ready, 8)

                def down(j):
                    wh, wl = chunk(f"fd{j}")
                    pe.wait_ge(hb_ready, 2 * j + 2)
                    for t in range(T):
                        for half in range(2):
                            for i in (2 * j, 2 * j + 1):
                                rows = slice(LASTROW if i == FT - 1 else 0, P)
                                w = slice((i - 2 * j) * D + half * 512, (i - 2 * j) * D + (half + 1) * 512)
                                m = three(ps[:, 3 + 2 * t + half, :], bTh[rows, i % K, t * P:(t + 1) * P], bTl[rows, i % K, t * P:(t + 1) * P],
                                          wh[rows, w], wl[rows, w], i == 0, i == FT - 1)
                    finish(f"fd{j}", m)

                for j in range(FG):
                    for half, name in enumerate((f"fg{j}", f"fu{j}")):
                        wh, wl = chunk(name)
                        for m_ in range(2):
                            i = 2 * j + m_
                            if half == 0 and i >= 3:
                                pe.wait_ge(hb_done, i - 2)
                            for k in range(K):
                                w = slice(k * 2 * P + m_ * P, k * 2 * P + (m_ + 1) * P)
                                m = three(ps[:, i % 3, half * SEQ:(half + 1) * SEQ], wh[:, w], wl[:, w], hTh[:, k, :], hTl[:, k, :],
                                          k == 0, k == K - 1)
                        finish(name, m)
                    if j:
                        down(j - 1)
                down(FG - 1)

            mixer(0)
            ffn()
            mixer(1)

            h_turn(3)
            pe.wait_ge(ht_ready, 16)
            pe.wait_ge(ada_used, summed[0])
            for t in range(T):
                for k in range(K):
                    m = pe.matmul(ps[:, 7, t * EXPERTS:(t + 1) * EXPERTS], hf[:, k, t * P:(t + 1) * P],
                                  col(COL_WR + k * EXPERTS, EXPERTS), start=(k == 0), stop=(k == K - 1))
            m.then_inc(router_full, 1)
            pe.wait_ge(sel_ready, 1)
            sel = r4[:, 2 * T * EXPERTS:3 * T * EXPERTS].rearrange("p (t e) -> p t e", t=T)
            for n, parts in enumerate((((before, 0),), ((ones, 0), (before, 1)), ((ones, 0), (ones, 1)))):
                for at, (w, t) in enumerate(parts):
                    m = pe.matmul(ps[:, 7, 32 + n * EXPERTS:32 + (n + 1) * EXPERTS], w[:, :], sel[:, t, :],
                                  start=(at == 0), stop=(at == len(parts) - 1))
            m.then_inc(count_full, 1)

            def gather(i, part):
                for kk in range(4):
                    k = 4 * part + kk
                    for t in range(T):
                        m = pe.matmul(ps[:, 7, kk * P:(kk + 1) * P], xn[:, t, k * P:(k + 1) * P], r4[:, t * P:(t + 1) * P],
                                      start=(t == 0), stop=(t == T - 1))
                m.then_inc(m_gath, 1)

            def item(i, par, first, ahead):
                def part(c):
                    pe.wait_ge(raw_done, i * PER_ITEM + (NR + c + 1))
                    return hi[:, (NW + c) % NSPLIT, :], lo[:, (NW + c) % NSPLIT, :]

                def up(kind, g):
                    for half in range(2):
                        wh, wl = part(spot(kind, g, half, first))
                        for kk in range(4):
                            k = 4 * half + kk
                            w = slice(kk * GRP, (kk + 1) * GRP)
                            at = slice(par * P, (par + 1) * P)
                            m = three(ps[:, (0 if kind == "w1" else 2) + g % 2, :], hTh[:, k, at], hTl[:, k, at],
                                      wh[:, w], wl[:, w], k == 0, k == K - 1)
                        m.then_inc(used, 1)

                if first:
                    pe.wait_ge(m_pos, i + 1)
                    pe.wait_ge(m_acc, i * 4 + 1)
                    gather(i, 0)
                    pe.wait_ge(m_xf, i * 2 + 1)
                    gather(i, 1)
                else:
                    pe.wait_ge(m_silu, i * NG)
                pe.wait_ge(m_x, i * 2 + 2)
                for g in range(NG):
                    up("w1", g)
                    if g:
                        turn(i, g - 1)
                    elif not first:
                        turn(i - 1, NG - 1)
                    if g == 1 and not first:
                        pe.wait_ge(m_yc, i)
                        scatter(i - 1, 0)
                    if g == 3:
                        pe.wait_ge(m_acc, i * 4 + 1)
                        for t in range(T):
                            m = pe.transpose(ps[:, 7, t * P:(t + 1) * P], r4[:, 256 + t * P:256 + (t + 1) * P], ident[:, :])
                        m.then_inc(m_gt, 1)
                    if ahead and g == NG - 2:
                        pe.wait_ge(m_gtc, i + 1)
                        pe.wait_ge(m_pos, i + 2)
                        gather(i + 1, 0)
                    if ahead and g == NG - 1:
                        pe.wait_ge(m_xf, i * 2 + 3)
                        gather(i + 1, 1)
                    up("w3", g)
                    if g in (1, 2) and not first:
                        scatter(i - 1, 2 * g - 1)
                    if g:
                        down(i, g - 1, spot("w2", g - 1, 0))
                    elif not first:
                        down(i - 1, NG - 1, spot("w2", NG - 1, 0))
                    if g == 1 and not first:
                        scatter(i - 1, 2)

            def turn(i, g):
                pe.wait_ge(m_hb, i * NG + g + 1)
                for c in range(4):
                    m = pe.transpose(ps[:, 6, c * P:(c + 1) * P], r3[:, HS[g] + c * P:HS[g] + (c + 1) * P], ident[:, :])
                m.then_inc(m_t, 1)

            def down(i, g, c0):
                pe.wait_ge(m_h, i * NG + g + 1)
                for half in range(2):
                    n = c0 + half
                    pe.wait_ge(raw_done, i * PER_ITEM + (NR + n + 1))
                    wh, wl = hi[:, (NW + n) % NSPLIT, :], lo[:, (NW + n) % NSPLIT, :]
                    for cc in range(2):
                        c = 2 * half + cc
                        for q in range(2):
                            w = slice(cc * D + q * 512, cc * D + (q + 1) * 512)
                            m = three(ps[:, 4 + q, :], bTh[:, c, 0:P], bTl[:, c, 0:P], wh[:, w], wl[:, w],
                                      g == 0 and c == 0, g == NG - 1 and c == 3)
                    m.then_inc(used, 1)

            def scatter(i, q):
                if q:
                    pe.wait_ge(m_acc, i * 4 + 1 + q)
                m = pe.matmul(ps[:, 7, :], r4[:, 512 + (q // 2) * P:512 + (q // 2 + 1) * P], r5[:, (q % 2) * 512:(q % 2 + 1) * 512],
                              start=True, stop=True)
                m.then_inc(m_sc, 1)

            def drain(i):
                turn(i, NG - 1)
                down(i, NG - 1, PER_ITEM - 2)
                pe.wait_ge(m_yc, i + 1)
                pe.wait_ge(m_gtc, i + 1)
                for q in range(4):
                    scatter(i, q)

            item(0, 0, True, True)
            with pe.Fori(0, EXPERTS // 2 - 1) as j:
                item(j * 2 + 1, 1, False, True)
                item(j * 2 + 2, 0, False, True)
            item(EXPERTS - 1, 1, False, False)
            drain(EXPERTS - 1)
            spare = pe.value_load(info[0:1, ITEMS:ITEMS + 1], min_val=0, max_val=SPARE)
            with pe.Fori(EXPERTS, ITEMS) as i:
                with pe.If(i < spare + EXPERTS):
                    item(i, 0, True, False)
                    drain(i)


OUT_SHAPE = (1, SEQ, D)


def rows_of(w, kc, tiles=None):
    *lead, k, n = w.shape
    w = w.reshape(*lead, k // (kc * P), kc, P, n)
    return np.ascontiguousarray(np.swapaxes(w, -3, -2)).reshape(*lead, k // (kc * P), P, kc * n)


def cols_of(w, c):
    *lead, k, n = w.shape
    w = np.moveaxis(w.reshape(*lead, k // P, P, n // c, c), -2, -4)
    return np.ascontiguousarray(np.swapaxes(w, -3, -2)).reshape(*lead, n // c, P, k // P * c)


def channels(v):
    return np.moveaxis(v.reshape(*v.shape[:-1], v.shape[-1] // P, P), -1, 0).reshape(P, -1)


def lay_out(i):
    w_in = i["w_in"]
    u, v, cq, kr, ga, gb = np.split(w_in, np.cumsum([GW, GW, QR, KVR + ROPE, D]), axis=-1)
    ukv = i["mla_w_ukv"].reshape(L, KVR, HEADS, NOPE + VD)
    ukv = np.concatenate([ukv[..., :NOPE].reshape(L, KVR, -1), ukv[..., NOPE:].reshape(L, KVR, -1)], -1)
    cut = (FT - 1) * P
    wide = lambda w: np.concatenate([w[..., :cut], w[..., -P:]], -1)
    w_fd = i["ffn_w_down"]
    fd = np.concatenate([w_fd[:, :cut], w_fd[:, -P:]], 1)
    w_ada = i["ada_w"].reshape(L, 4, 2, P, 6, D).transpose(0, 4, 1, 3, 2, 5).reshape(L, 6, 4, P, CH)
    up = lambda w: np.ascontiguousarray(
        w[0].reshape(EXPERTS, 2, 4, P, NG, GRP).transpose(0, 4, 1, 3, 2, 5)).reshape(EXPERTS, NG, 2, P, CH)
    pack = np.concatenate([
        channels(i["c"]), channels(i["ada_b"]),
        channels(np.stack([i["norm_mix_pre"], i["norm_ffn_pre"]], 1)),
        channels(i["mla_q_norm"]), channels(i["mla_kv_norm"]),
        i["gmlp_bs"].transpose(2, 0, 1).reshape(P, -1),
        i["moe_router"][0].reshape(K, P, EXPERTS).transpose(1, 0, 2).reshape(P, -1)], 1)
    return {
        "x": i["x"], "cols": pack, "positions": i["positions"][0].reshape(T, P).T, "router_bias": i["moe_router_bias"],
        "ln_g": i["gmlp_ln_g"], "ln_b": i["gmlp_ln_b"], "post_m": i["norm_mix_post"], "post_f": i["norm_ffn_post"],
        "ws": i["gmlp_ws"].transpose(0, 3, 1, 2).reshape(L, P, GROUPS * P),
        "w_ada": w_ada, "w_cq": rows_of(cq, 4), "w_kr": rows_of(kr, 4), "w_v": rows_of(v, 4), "w_u": rows_of(u, 4),
        "w_uq": cols_of(i["mla_w_uq"], QR), "w_ukv": rows_of(ukv, KC),
        "w_ga": cols_of(ga, 2 * P), "w_gb": cols_of(gb, 2 * P),
        "w_ab": cols_of(np.concatenate([i["w_branch_a"], i["w_branch_b"]], 1), 2 * P), "w_o": rows_of(i["w_out"], 2),
        "w_fg": cols_of(wide(i["ffn_w_gate"]), 2 * P), "w_fu": cols_of(wide(i["ffn_w_up"]), 2 * P), "w_fd": rows_of(fd, 2),
        "moe_w1": up(i["moe_w1"]), "moe_w3": up(i["moe_w3"]),
        "moe_w2": rows_of(i["moe_w2"][0], 2).reshape(EXPERTS, NG, 2, P, CH),
    }


def kernel(**inputs):
    import concourse.bacc as _bacc
    from concourse.bass_utils import run_bass_kernel_spmd as _run

    nc = _bacc.Bacc("TRN2", target_bir_lowering=False, num_devices=1)
    arrays, args = {}, {}
    for name, a in lay_out({k: np.asarray(v) for k, v in inputs.items()}).items():
        a = np.ascontiguousarray(a)
        arrays[f"in_{name}_dram"] = a
        args[name] = nc.dram_tensor(f"in_{name}_dram", a.shape, mybir.dt.from_np(a.dtype), kind="ExternalInput").ap()
    out = nc.dram_tensor("out_0_dram", OUT_SHAPE, f32, kind="ExternalOutput").ap()
    build(nc, args, out)
    r = _run(nc, [arrays], core_ids=[0])
    return r.results[0]["out_0_dram"]
```

```python
from contextlib import ExitStack

import numpy as np
import concourse.bass as bass
from concourse import mybir

P = 128
D = 1024
SEQ = 256
T = SEQ // P
K = D // P
L = 2
GROUPS, GDIM = 8, 64
GW = GROUPS * GDIM
HEADS, NOPE, ROPE, VD = 8, 64, 32, 64
QKD = NOPE + ROPE
QR, KVR = 384, 256
QC, KC = QR // P, KVR // P
LATC = QC + KC
HALF = ROPE // 2
THETA = 10000.0
FF_DENSE = 2752
FT = (FF_DENSE + P - 1) // P
FG = FT // 2
LASTROW = (FT * P - FF_DENSE)
EXPERTS = 8
FF_EXP = 3584
GRP = 512
NG = FF_EXP // GRP
SPARE = 3
ITEMS = EXPERTS + SPARE
CH = 2048
NRAW, NSPLIT = 7, 3
PER_ITEM = 6 * NG
EPS = 1e-6
NEG = -1.0e30
LAG_SUM, LAG_USE = 3, 6

f32 = mybir.dt.float32
f32r = mybir.dt.float32r
i32 = mybir.dt.int32
ALU = mybir.AluOpType
ACT = mybir.ActivationFunctionType
AX = mybir.AxisListType.X

SH_M, SC_M, G_M, SH_F, SC_F, G_F = range(6)

COL_C = 0
COL_ADA = COL_C + K
COL_NORM = COL_ADA + L * 6 * K
COL_QN = COL_NORM + L * 2 * K
COL_KVN = COL_QN + L * QC
COL_BS = COL_KVN + L * KC
COL_WR = COL_BS + L * GROUPS
COLS = COL_WR + K * EXPERTS


def mixer_chunks(l):
    out = [(f"cq{h}", "w_cq", (l, h), 4 * QR) for h in range(2)]
    out += [(f"kr{h}", "w_kr", (l, h), 4 * (KVR + ROPE)) for h in range(2)]
    out += [(f"v{h}", "w_v", (l, h), 4 * GW) for h in range(2)]
    out += [(f"u{h}", "w_u", (l, h), 4 * GW) for h in range(2)]
    out += [(f"uq{h}", "w_uq", (l, h), QC * QR) for h in range(2)]
    out += [("ukv", "w_ukv", (l, 0), CH)]
    for j in range(4):
        out += [(f"ga{j}", "w_ga", (l, j), CH), (f"gb{j}", "w_gb", (l, j), CH), (f"ab{j}", "w_ab", (l, j), CH)]
    out += [(f"wo{j}", "w_o", (l, j), CH) for j in range(4)]
    return [((f"m{l}." + n), t, i, e) for n, t, i, e in out]


def ffn_chunks():
    out = []
    for j in range(FG):
        out += [(f"fg{j}", "w_fg", (0, j), CH), (f"fu{j}", "w_fu", (0, j), CH)]
        if j:
            out.append((f"fd{j - 1}", "w_fd", (0, j - 1), CH))
    return out + [(f"fd{FG - 1}", "w_fd", (0, FG - 1), CH)]


WEIGHTS = mixer_chunks(0) + ffn_chunks() + mixer_chunks(1)
CHUNK = {name: s for s, (name, _, _, _) in enumerate(WEIGHTS)}
NW = len(WEIGHTS)
M0, F0, M1 = 0, len(mixer_chunks(0)), len(mixer_chunks(0)) + len(ffn_chunks())
ADA_FIRST = [(0, SH_M), (0, SC_M)]
ADA_AT = [(0, G_M, M0 + 2), (0, SH_F, M0 + 9), (0, SC_F, M0 + 16),
          (1, SH_M, F0), (1, SC_M, F0 + 6), (0, G_F, F0 + 12), (1, G_M, F0 + 21),
          (1, SH_F, M1), (1, SC_F, M1 + 6), (1, G_F, M1 + 12)]
ADA = ADA_FIRST + [(l, v) for l, v, _ in ADA_AT]


def stream():
    out = [("ada", a, q) for a in range(len(ADA_FIRST)) for q in range(4)]
    for s in range(NW):
        for a, (_, _, at) in enumerate(ADA_AT):
            if at <= s < at + 4:
                out.append(("ada", len(ADA_FIRST) + a, s - at))
        out.append(("w", s, 0))
    return out


STREAM = stream()
RAW_OF = {(kind, n, q): r for r, (kind, n, q) in enumerate(STREAM)}
NR = len(STREAM)


def ada_sums():
    out = []
    for a, (_, v, at) in enumerate(ADA_AT, len(ADA_FIRST)):
        for half in range(2 if v in (G_M, G_F) else 1):
            out.append((a, half, at + LAG_SUM * (1 + half), at + LAG_USE + LAG_SUM * half))
    return out


SUMS = ada_sums()


def spot(kind, g, half=1, first=False):
    if kind == "w2":
        c = 6 * (g + 1) + 4 + half
    else:
        c = 6 * g + (0 if kind == "w1" else 2) + half
    return c if first and c < 4 else c - 2


def item_order(first):
    out = []
    for g in range(NG):
        out += [(spot(kind, g, h, first), kind, g, h, False) for kind in ("w1", "w3") for h in range(2)]
        if g:
            out += [(spot("w2", g - 1, h), "w2", g - 1, h, False) for h in range(2)]
        elif not first:
            out += [(spot("w2", -1, h), "w2", NG - 1, h, True) for h in range(2)]
    return out


LAST = [(PER_ITEM - 2 + h, "w2", NG - 1, h, False) for h in range(2)]
DRAIN = (7, 0, 1, 2)


Y_BANK = [(0, 2), (3, 5), (0, 2)]
X_BANKS = [(0, 1, 2, 3), (4, 5, 6, 3)] * 2
R_BANK = (7, 2)


def build(nc, A, out):
    with ExitStack() as ctx:
        def sb(name, shape, dt=f32):
            return ctx.enter_context(nc.sbuf_tensor(name, shape, dt))

        def sem(name):
            return ctx.enter_context(nc.semaphore(name))

        raw = sb("raw", [P, NRAW, CH])
        hi = sb("hi", [P, NSPLIT, CH], f32r)
        lo = sb("lo", [P, NSPLIT, CH], f32r)
        x = sb("x_tok", [P, T, D])
        r2 = sb("r2", [P, T * D])
        r3 = sb("r3", [P, T * D])
        r4 = sb("r4", [P, 4 * 512])
        r5 = sb("r5", [P, T * HEADS * VD])
        r6 = sb("r6", [P, 2 * HEADS * SEQ])
        r7 = sb("r7", [P, D])
        gate_m = sb("gate_m", [P, D])
        acc = sb("ada_acc", [P, D])
        hTh, hTl = (sb(n, [P, K, SEQ], f32r) for n in ("hT_hi", "hT_lo"))
        bTh, bTl = (sb(n, [P, K, SEQ], f32r) for n in ("bT_hi", "bT_lo"))
        cols = sb("cols", [P, COLS])
        cact = sb("silu_c", [P, K])
        AB = sb("scale_shift", [P, 2 * L, 2, K])
        ident = sb("ident", [P, P])
        ones = sb("ones", [P, P])
        before = sb("before", [P, P])
        mask = sb("mask", [P, 2 * P])
        slots = sb("slots", [P, P])
        pos_i, posf = sb("pos_i", [P, T], i32), sb("posf", [P, T])
        inv = sb("inv_freq", [P, HALF])
        cosT, sinT = (sb(n, [P, T, HALF]) for n in ("cos", "sin"))
        ms, rstd = sb("mean_sq", [P, 4]), sb("rstd", [P, 4])
        bn, mv = sb("bn", [P, T, 6]), sb("mean_var", [P, T, 2])
        small = sb("small", [P, 4])
        warm = sb("warm", [P, 1])
        mx, nmx = sb("mx", [P, 6, 4]), sb("neg_max", [P, 6, 4])
        psum_p, rinv = sb("sum_p", [P, 6, 4]), sb("rinv", [P, T, HEADS])
        rope_t = sb("rope_t", [P, 2, T * HALF])
        lt_mask = sb("lt_mask", [P, EXPERTS, EXPERTS])
        spare_no = sb("spare_no", [P, SPARE, EXPERTS])
        rb = sb("router_bias", [P, EXPERTS])
        eidx = sb("expert_idx", [P, EXPERTS])
        pos_tab, gate_tab = (sb(n, [P, T, ITEMS]) for n in ("pos_tab", "gate_tab"))
        pg = sb("pg", [P, 2, T])
        info = sb("info", [P, ITEMS + 1], i32)
        ps = ctx.enter_context(nc.psum_tensor("ps", [P, 8, 512], f32))

        y_sb = r2[:, :].rearrange("p (t d) -> p t d", t=T)
        v_g = r2[:, 0:T * GW].rearrange("p (t d) -> p t d", t=T)
        u_g = r2[:, T * GW:2 * T * GW].rearrange("p (t d) -> p t d", t=T)
        scratch = r3[:, 0:T * D].rearrange("p (t d) -> p t d", t=T)
        hf = r3[:, 0:K * SEQ].rearrange("p (k s) -> p k s", k=K)
        NQ = T * (HEADS + 1) * QKD
        qk = r3[:, 0:NQ].rearrange("p (t h d) -> p t h d", t=T, h=HEADS + 1)
        k_tok = r4[:, 0:T * HEADS * QKD].rearrange("p (t h d) -> p t h d", t=T, h=HEADS)
        pT = r3[:, 0:4 * 512].rearrange("p (u s) -> p u s", u=4)
        lat = r4[:, 0:T * LATC * P].rearrange("p (t d) -> p t d", t=T)
        S = r4[:, :].rearrange("p (u s) -> p u s", u=4)
        v_tok = r5[:, :].rearrange("p (t d) -> p t d", t=T)
        qT = r6[0:QKD, 0:HEADS * SEQ].rearrange("p (h s) -> p h s", h=HEADS)
        kT = r6[0:QKD, HEADS * SEQ:2 * HEADS * SEQ].rearrange("p (h s) -> p h s", h=HEADS)
        ln_g, ln_b = r6[:, HEADS * SEQ:HEADS * SEQ + GW], r6[:, HEADS * SEQ + GW:HEADS * SEQ + 2 * GW]
        o_tok = r6[:, 0:T * GW].rearrange("p (t d) -> p t d", t=T)
        merged = r6[:, HEADS * SEQ:2 * HEADS * SEQ].rearrange("p (k s) -> p k s", k=K)
        y_exp = r6[:, 0:T * D].rearrange("p (t d) -> p t d", t=T)
        ws = r7[:, :].rearrange("p (g t) -> p g t", g=GROUPS)
        gate_f = r7

        diag = r4[:, 4 * 512 - T * P:].rearrange("p (t s) -> p t s", t=T)
        slots_i, eidx_i = r4[:, 0:P].bitcast(i32), r4[:, P:P + EXPERTS].bitcast(i32)
        ang = r4[:, 2 * P:2 * P + T * HALF].rearrange("p (t d) -> p t d", t=T)

        hs = [(r2 if g == NG - 1 else r3)[:, at:at + GRP] for g in range(NG)
              for at in [0 if g == NG - 1 else 1024 + GRP * (g % 2)]]

        def col(at, n=1):
            return cols[:, at:at + n]

        consts_in, small_in = sem("consts_in"), sem("small_in")
        x_in = sem("x_in")
        raw_full = [sem(f"raw_full{i}") for i in range(NRAW)]
        hi_done = sem("hi_done")
        raw_done = sem("raw_done")
        used = sem("used")
        ws_in, ln_in, post_m_in, post_f_in = (sem(n) for n in ("ws_in", "ln_in", "post_m_in", "post_f_in"))
        pool_setup, ws_masked = sem("pool_setup"), sem("ws_masked")
        cact_ready = sem("cact_ready")
        ada_acc, ada_full, ada_used = sem("ada_acc"), sem("ada_full"), sem("ada_used")
        ang_ready, rope_ready = sem("ang_ready"), sem("rope_ready")
        var_ready, rstd_ready = sem("var_ready"), sem("rstd_ready")
        sq_done, diag_ready, xt_full = (sem(n) for n in ("sq_done", "diag_ready", "xt_full"))
        hf_ready, hth_ready, ht_ready = sem("hf_ready"), sem("hth_ready"), sem("ht_ready")
        lat_copied, vu_done, lat_ready, latT_full = (sem(n) for n in ("lat_copied", "vu_done", "lat_ready", "latT_full"))
        latTh_ready, latT_ready = sem("latTh_ready"), sem("latT_ready")
        attn_copied, qk_ready = sem("attn_copied"), sem("qk_ready")
        qT_full, kT_full, qT_copied, kT_copied = (sem(n) for n in ("qT_full", "kT_full", "qT_copied", "kT_copied"))
        vn_ready, z_full, uz_ready = sem("vn_ready"), sem("z_full"), sem("uz_ready")
        sc_full, s_ready, nmx_ready, p_ready = (sem(n) for n in ("sc_full", "s_ready", "nmx_ready", "p_ready"))
        pT_full, pT_copied, o_full, o_ready = (sem(n) for n in ("pT_full", "pT_copied", "o_full", "o_ready"))
        brT_full, brTh_ready, brT_ready = sem("brT_full"), sem("brTh_ready"), sem("brT_ready")
        sig_done, mg_done, mth_ready, mt_ready = (sem(n) for n in ("sig_done", "mg_done", "mth_ready", "mt_ready"))
        y_full, x_done, sum_ready = sem("y_full"), sem("x_done"), sem("sum_ready")
        silu_done, hb_done, hbh_ready, hb_ready = (sem(n) for n in ("silu_done", "hb_done", "hbh_ready", "hb_ready"))
        router_full, ex_in, ex_done, sel_ready, count_full, pos_ready, gates_ready, route_ready = (
            sem(n) for n in ("router_full", "ex_in", "ex_done", "sel_ready", "count_full", "pos_ready", "gates_ready",
                             "route_ready"))
        m_pos, m_gath, m_xf, m_xh, m_x = (sem(n) for n in ("m_pos", "m_gath", "m_xf", "m_xh", "m_x"))
        m_gt, m_gtc, m_silu, m_hb, m_t, m_hh, m_h = (sem(n) for n in ("m_gt", "m_gtc", "m_silu", "m_hb", "m_t", "m_hh", "m_h"))
        m_yc, m_sc, m_acc = sem("m_yc"), sem("m_sc"), sem("m_acc")
        out_done = sem("out_done")
        v_step, v_loop = sem("v_step"), sem("v_loop")
        p_step = sem("p_step")

        block = ctx.enter_context(nc.Block())

        @block.sync
        def _(sp):
            sp.dma_start(cols[:, :], A["cols"]).then_inc(consts_in, 16)
            for r, (kind, n, q) in enumerate(STREAM):
                if r >= NRAW:
                    sp.wait_ge(raw_done, r - NRAW + 1)
                if kind == "ada":
                    l, v = ADA[n]
                    src, e = A["w_ada"][l, v, q], CH
                else:
                    _, t, (a, b), e = WEIGHTS[n]
                    src = A[t][a, b]
                sp.dma_start(raw[:, r % NRAW, 0:e], src).then_inc(raw_full[r % NRAW], 16)
                if r == NRAW - 2:
                    sp.dma_start(x[:, :, :], A["x"].rearrange("b (t p) d -> p (b t) d", p=P)).then_inc(x_in, 16)

            def item_loads(i, chunks, expert):
                for c, kind, g, half, before_ in chunks:
                    sp.wait_ge(raw_done, i * PER_ITEM + (NR + c - NRAW + 1))
                    e = expert - 1 if before_ else expert
                    src = A["moe_" + kind]
                    src = src[e, g, half] if isinstance(e, int) else \
                        src[bass.ds(e, 1), g, half, :, :].rearrange("e p n -> p (e n)")
                    slot = (NR + c) % NRAW
                    sp.dma_start(raw[:, slot, :], src).then_inc(raw_full[slot], 16)

            item_loads(0, item_order(True), 0)
            with sp.Fori(1, EXPERTS) as i:
                item_loads(i, item_order(False), i)
            item_loads(EXPERTS - 1, LAST, EXPERTS - 1)
            sp.wait_ge(route_ready, 1)
            spare = sp.value_load(info[0:1, ITEMS:ITEMS + 1], min_val=0, max_val=SPARE)
            with sp.If(spare > 0):
                with sp.Fori(EXPERTS, ITEMS) as i:
                    with sp.If(i < spare + EXPERTS):
                        expert = sp.value_load(info[0:1, bass.ds(i, 1)], min_val=0, max_val=EXPERTS - 1)
                        item_loads(i, item_order(True) + LAST, expert)
            for t in range(T):
                sp.wait_ge(x_done, 2 * L * T - T + 1 + t)
                sp.dma_start(out[0, t * P:(t + 1) * P, :], x[:, t, :]).then_inc(out_done, 16)
            sp.wait_ge(out_done, 16 * T)

        @block.gpsimd
        def _(pool):
            pool.dma_start(pos_i[:, :], A["positions"]).then_inc(small_in, 16)
            pool.dma_start(rb[:, :], A["router_bias"].to_broadcast([P, EXPERTS])).then_inc(small_in, 16)

            def load_ws(l):
                pool.dma_start(r7[:, :], A["ws"][l]).then_inc(ws_in, 16)

            def load_ln(l):
                pool.dma_start(ln_g, A["ln_g"][l:l + 1].to_broadcast([P, GW])).then_inc(ln_in, 16)
                pool.dma_start(ln_b, A["ln_b"][l:l + 1].to_broadcast([P, GW])).then_inc(ln_in, 16)

            def load_post(dst, name, l, s):
                pool.dma_start(dst[:, :], A[name][l:l + 1].to_broadcast([P, D])).then_inc(s, 16)

            def mask_ws(l):
                pool.wait_ge(ws_in, 16 * (l + 1))
                pool.affine_select(out=ws, in_=ws, compare_op=ALU.is_ge, fill=0.0, base=0,
                                   pattern=[[0, GROUPS], [1, P]], channel_multiplier=-1).then_inc(ws_masked, 1)

            pool.memset(warm[:, :], 1.0).then_inc(p_step, 1)
            pool.memset(ident[:, :], 0.0).then_inc(p_step, 1)
            pool.memset(ones[:, :], 1.0).then_inc(p_step, 1)
            pool.memset(before[:, :], 1.0).then_inc(p_step, 1)
            pool.memset(mask[:, :], 0.0).then_inc(p_step, 1)
            pool.memset(lt_mask[:, :, :], 1.0).then_inc(p_step, 1)
            for j in range(SPARE):
                pool.memset(spare_no[:, j, :], float(j)).then_inc(p_step, 1)
            for f in range(HALF):
                value = float(np.float32(1.0) / np.float32(THETA) ** np.float32(2.0 * f / ROPE))
                pool.memset(inv[:, f:f + 1], value).then_inc(p_step, 1)
            pool.iota(slots_i, pattern=[[1, P]], base=0, channel_multiplier=0).then_inc(p_step, 1)
            pool.iota(eidx_i, pattern=[[1, EXPERTS]], base=0, channel_multiplier=0).then_inc(p_step, 1)
            pool.wait_ge(p_step, 8 + SPARE + HALF)
            pool.affine_select(out=ident[:, :], in_=ident[:, :], compare_op=ALU.not_equal, fill=1.0, base=0,
                               pattern=[[-1, P]], channel_multiplier=1).then_inc(pool_setup, 1)
            pool.affine_select(out=before[:, :], in_=before[:, :], compare_op=ALU.is_gt, fill=0.0, base=0,
                               pattern=[[1, P]], channel_multiplier=-1).then_inc(pool_setup, 1)
            pool.affine_select(out=mask[:, P:2 * P], in_=mask[:, P:2 * P], compare_op=ALU.is_ge, fill=NEG, base=0,
                               pattern=[[-1, P]], channel_multiplier=1).then_inc(pool_setup, 1)
            pool.affine_select(out=lt_mask[:, :, :], in_=lt_mask[:, :, :], compare_op=ALU.is_gt, fill=0.0, base=0,
                               pattern=[[1, EXPERTS], [-1, EXPERTS]], channel_multiplier=0).then_inc(pool_setup, 1)
            pool.tensor_copy(slots[:, :], slots_i).then_inc(pool_setup, 1)
            pool.tensor_copy(eidx[:, :], eidx_i).then_inc(pool_setup, 1)
            def link(ins):
                steps[0] += 1
                ins.then_inc(p_step, 1)
                pool.wait_ge(p_step, steps[0])

            steps = [8 + SPARE + HALF]
            TWO_PI = 2.0 * np.pi
            C1 = 6.28125
            C2 = float(np.round((TWO_PI - C1) * 2 ** 20) / 2 ** 20)
            C3 = float(TWO_PI - C1 - C2)
            BIG = 1.5 * 2.0 ** 23
            LIMIT = float(np.nextafter(np.float32(np.pi), np.float32(0)))
            pool.wait_ge(small_in, 32)
            link(pool.tensor_copy(posf[:, :], pos_i[:, :]))
            for t in range(T):
                m = pool.tensor_scalar(ang[:, t, :], inv[:, :], posf[:, t:t + 1], None, ALU.mult)
            link(m)
            for dst, quarter in ((cosT, 0.25), (sinT, 0.0)):
                r, turn = (rope_t[:, z, 0:T * HALF].rearrange("p (t d) -> p t d", t=T) for z in range(2))
                link(pool.tensor_scalar(dst[:, :, :], ang[:, :, :], 1.0 / TWO_PI, quarter, ALU.mult, ALU.add))
                link(pool.tensor_scalar(dst[:, :, :], dst[:, :, :], BIG, None, ALU.add))
                link(pool.tensor_scalar(dst[:, :, :], dst[:, :, :], -BIG, None, ALU.add))
                for c, src in ((C1, ang[:, :, :]), (C2, r), (C3, r)):
                    link(pool.tensor_scalar(turn, dst[:, :, :], -c, None, ALU.mult))
                    link(pool.tensor_tensor(r, src, turn, ALU.add))
                link(pool.tensor_scalar(r, r, quarter * TWO_PI, LIMIT, ALU.add, ALU.min))
                m = pool.tensor_scalar(dst[:, :, :], r, -LIMIT, None, ALU.max)
                if dst is cosT:
                    link(m)
            m.then_inc(ang_ready, 1)

            pool.wait_ge(raw_done, RAW_OF["ada", 1, 3])
            load_post(gate_m, "post_m", 0, post_m_in)
            load_ln(0)
            load_ws(0)
            mask_ws(0)
            pool.wait_ge(z_full, T)
            load_post(gate_f, "post_f", 0, post_f_in)
            pool.wait_ge(x_done, T)
            load_post(gate_m, "post_m", 1, post_m_in)
            pool.wait_ge(x_done, 2 * T)
            load_ws(1)
            load_ln(1)
            mask_ws(1)
            pool.wait_ge(z_full, 2 * T)
            load_post(gate_f, "post_f", 1, post_f_in)
            pool.wait_ge(mt_ready, 2 * T)
            pool.memset(r6[:, 0:T * D], 0.0).then_inc(m_acc, 1)

        @block.scalar
        def _(act):
            done = [0]

            def hi_part(s):
                r = RAW_OF["w", s, 0]
                e = WEIGHTS[s][3]
                act.wait_ge(raw_full[r % NRAW], 16 * (r // NRAW + 1))
                if s >= NSPLIT:
                    act.wait_ge(used, s - NSPLIT + 1)
                act.activation(hi[:, s % NSPLIT, 0:e], raw[:, r % NRAW, 0:e], ACT.Copy).then_inc(hi_done, 1)

            def upto(name, ahead=2):
                while done[0] < min(CHUNK[name] + ahead + 1, NW):
                    hi_part(done[0])
                    done[0] += 1

            def need(name):
                act.wait_ge(used, CHUNK[name] + 1)

            def item_hi(i, lo_c, hi_c):
                for c in range(lo_c, hi_c):
                    slot, s = (NR + c) % NRAW, (NW + c) % NSPLIT
                    act.wait_ge(raw_full[slot], i * (16 * PER_ITEM // NRAW) + 16 * ((NR + c) // NRAW + 1))
                    act.wait_ge(used, i * PER_ITEM + (NW + c - NSPLIT + 1))
                    act.activation(hi[:, s, :], raw[:, slot, :], ACT.Copy).then_inc(hi_done, 1)

            roots, xs = [0], [0]

            def root(n, at=0):
                roots[0] += 1
                act.wait_ge(var_ready, roots[0])
                act.activation(rstd[:, at:at + n], ms[:, at:at + n], ACT.Sqrt).then_inc(rstd_ready, 1)

            def square(src, t, at):
                act.activation(scratch[:, t, :].rearrange("p (c s) -> p c s", c=2), src, ACT.Square, scale=D ** -0.5,
                               accum_out=ms[:, at:at + 1]).then_inc(sq_done, 1)

            def x_norm():
                for t in range(T):
                    xs[0] += 1
                    if xs[0] > T:
                        act.wait_ge(x_done, xs[0] - T)
                    square(x[:, t, :].rearrange("p (c s) -> p c s", c=2), t, T + t)
                    root(1, T + t)

            def y_norm(n, name):
                for t in range(T):
                    if t == 0:
                        act.wait_ge(y_full, n + 1)
                    else:
                        need(name)
                    square(ps[:, Y_BANK[n][t]:Y_BANK[n][t] + 2, :], t, t)
                    root(1, t)

            def h_hi(n):
                for b in range(4):
                    act.wait_ge(hf_ready, 4 * n + b + 1)
                    act.activation(hTh[:, 2 * b:2 * b + 2, :], hf[:, 2 * b:2 * b + 2, :], ACT.Copy).then_inc(hth_ready, 1)

            act.wait_ge(consts_in, 16)
            act.activation(cact[:, :], cols[:, COL_C:COL_C + K], ACT.Silu).then_inc(cact_ready, 1)
            act.wait_ge(p_step, 1)
            act.activation(warm[:, :], warm[:, :], ACT.Sqrt)
            act.wait_ge(x_in, 16)
            x_norm()
            act.wait_ge(ang_ready, 1)
            act.activation(cosT[:, :, :], cosT[:, :, :], ACT.Sin)
            act.activation(sinT[:, :, :], sinT[:, :, :], ACT.Sin).then_inc(rope_ready, 1)

            def mixer(l):
                if l == 0:
                    upto("m0.cq0", 1)
                h_hi(2 * l)
                upto(f"m{l}.cq1")
                need(f"m{l}.cq1")
                for t in range(T):
                    act.activation(lat[:, t, 0:QR], ps[:, 4 + t, 0:QR], ACT.Copy).then_inc(lat_copied, 1)
                upto(f"m{l}.kr1")
                need(f"m{l}.kr1")
                for t in range(T):
                    bank = [6, 0][t]
                    act.activation(lat[:, t, QR:QR + KVR], ps[:, bank, 0:KVR], ACT.Copy)
                    act.activation(qk[:, t, HEADS, NOPE:QKD], ps[:, bank, KVR:KVR + ROPE], ACT.Copy).then_inc(lat_copied, 1)
                root(2 * T)
                upto(f"m{l}.v1")
                need(f"m{l}.v1")
                for t in range(T):
                    act.activation(v_g[:, t, :], ps[:, 1 + t, :], ACT.Gelu).then_inc(vu_done, 1)
                for kk in range(LATC):
                    act.wait_ge(latT_full, 3 * l + kk // 2 + 1)
                    at = COL_QN + l * QC + kk if kk < QC else COL_KVN + l * KC + kk - QC
                    act.activation(bTh[:, kk, :], ps[:, [5, 6, 0][kk // 2], (kk % 2) * SEQ:(kk % 2 + 1) * SEQ],
                                   ACT.Identity, scale=col(at)).then_inc(latTh_ready, 1)
                root(T)
                upto(f"m{l}.u1")
                need(f"m{l}.u1")
                for t in range(T):
                    act.activation(u_g[:, t, :], ps[:, 3 + t, :], ACT.Gelu).then_inc(vu_done, 1)
                for h in range(2):
                    upto(f"m{l}.uq{h}")
                    need(f"m{l}.uq{h}")
                    for t in range(T):
                        act.activation(qk[:, t, 4 * h:4 * h + 4, :],
                                       ps[:, [5, 6, 0, 1][2 * h + t], 0:QR].rearrange("p (h d) -> p h d", h=4),
                                       ACT.Copy).then_inc(attn_copied, 1)
                upto(f"m{l}.ukv")
                need(f"m{l}.ukv")
                for t in range(T):
                    act.activation(k_tok[:, t, :, 0:NOPE], ps[:, 2 + t, :].rearrange("p (h d) -> p h d", h=HEADS),
                                   ACT.Copy).then_inc(attn_copied, 1)
                for t in range(T):
                    act.activation(v_tok[:, t, :], ps[:, 4 + t, :], ACT.Copy).then_inc(attn_copied, 1)
                for j in range(4):
                    act.wait_ge(qT_full, 4 * l + j + 1)
                    act.activation(qT[:, 2 * j:2 * j + 2, :],
                                   ps[0:QKD, [6, 0, 1, 2][j], :].rearrange("p (h s) -> p h s", h=2),
                                   ACT.Copy).then_inc(qT_copied, 1)

                def exps(u):
                    heads, keys = (4, P) if u < 2 else (2, SEQ)
                    act.wait_ge(nmx_ready, 6 * l + u + 1)
                    for h in range(heads):
                        m = act.activation(S[:, u % 4, h * keys:(h + 1) * keys], S[:, u % 4, h * keys:(h + 1) * keys],
                                           ACT.Exp, bias=nmx[:, u, h:h + 1], scale=QKD ** -0.5,
                                           accum_out=psum_p[:, u, h:h + 1])
                    m.then_inc(p_ready, 1)

                def copy_pT(u):
                    act.wait_ge(pT_full, 6 * l + u + 1)
                    if u >= 4:
                        act.wait_ge(o_full, T * l + 1)
                    act.activation(pT[:, u % 4, :], ps[:, 1 + u, :], ACT.Copy).then_inc(pT_copied, 1)

                for step, u in ((exps, 0), (exps, 1), (copy_pT, 0), (exps, 2), (copy_pT, 1), (exps, 3), (copy_pT, 2),
                                (copy_pT, 3), (exps, 4), (exps, 5), (copy_pT, 4), (copy_pT, 5)):
                    step(u)
                for i in range(2 * T):
                    t = i % T
                    act.wait_ge(brT_full, 4 * l + i + 1)
                    act.activation(bTh[:, 4 * (i // T):4 * (i // T) + 4, t * P:(t + 1) * P],
                                   ps[:, [4, 5, 6, 0][i], :].rearrange("p (c s) -> p c s", c=4),
                                   ACT.Copy).then_inc(brTh_ready, 1)
                for j in range(4):
                    upto(f"m{l}.gb{j}")
                    need(f"m{l}.gb{j}")
                    for m in range(2):
                        mm = 2 * j + m
                        if mm >= 4:
                            act.wait_ge(mg_done, 8 * l + mm - 3)
                        act.activation(S[:, mm % 4, :], ps[:, 1 + m, :], ACT.Sigmoid).then_inc(sig_done, 1)
                    upto(f"m{l}.ab{j}")
                for h in range(2):
                    act.wait_ge(mg_done, 8 * l + 4 * h + 4)
                    act.activation(hTh[:, 4 * h:4 * h + 4, :], merged[:, 4 * h:4 * h + 4, :], ACT.Copy).then_inc(mth_ready, 1)
                act.activation(warm[:, :], warm[:, :], ACT.Sqrt)
                upto(f"m{l}.wo3")
                if l == L - 1:
                    item_hi(0, 0, 2)
                y_norm(2 * l, f"m{l}.wo3")
                x_norm()

            def ffn():
                h_hi(1)
                for j in range(FG):
                    upto(f"fu{j}")
                    need(f"fu{j}")
                    for i in (2 * j, 2 * j + 1):
                        if i >= 4:
                            act.wait_ge(hb_ready, i - 3)
                        act.activation(r4[:, (i % 4) * SEQ:(i % 4 + 1) * SEQ], ps[:, i % 3, 0:SEQ], ACT.Silu).then_inc(silu_done, 1)
                    for i in (2 * j, 2 * j + 1):
                        act.wait_ge(hb_done, i + 1)
                        if i >= K:
                            act.wait_ge(used, CHUNK[f"fd{(i - K) // 2}"] + 1)
                        act.activation(bTh[:, i % K, :], r4[:, (i % 4) * SEQ:(i % 4 + 1) * SEQ], ACT.Copy).then_inc(hbh_ready, 1)
                act.activation(warm[:, :], warm[:, :], ACT.Sqrt)
                upto(f"fd{FG - 1}")
                y_norm(1, f"fd{FG - 1}")
                x_norm()

            mixer(0)
            ffn()
            mixer(1)

            h_hi(3)
            act.activation(warm[:, :], warm[:, :], ACT.Exp)
            item_hi(0, 2, 3)
            act.wait_ge(ex_in, 1)
            act.activation(r4[:, 1024:1024 + T * EXPERTS], r4[:, 1024:1024 + T * EXPERTS], ACT.Exp).then_inc(ex_done, 1)

            def gather_hi(i, par, h):
                act.wait_ge(m_xf, i * 2 + h + 1)
                act.activation(hTh[:, 4 * h:4 * h + 4, par * P:(par + 1) * P],
                               r3[:, 512 * h:512 * h + 512].rearrange("p (k s) -> p k s", k=4), ACT.Copy).then_inc(m_xh, 1)

            def hidden_hi(i, g):
                act.wait_ge(m_t, i * NG + g + 1)
                act.activation(bTh[:, 0:4, 0:P], ps[:, 6, :].rearrange("p (c s) -> p c s", c=4), ACT.Copy).then_inc(m_hh, 1)

            def copy_y(i, last):
                act.wait_ge(used, i * PER_ITEM + (NW + last + 1))
                act.activation(r5[:, :].rearrange("p (c s) -> p c s", c=2), ps[:, 4:6, :], ACT.Copy).then_inc(m_yc, 1)

            def item(i, par, first, ahead):
                if first:
                    for h in range(2):
                        gather_hi(i, par, h)
                    if not ahead:
                        item_hi(i, 0, 2)
                at = [(3 if ahead else 2) if first else 0]

                def upto_c(c):
                    item_hi(i, at[0], c + 1)
                    at[0] = max(at[0], c + 1)

                for g in range(NG):
                    c = spot("w1", g, 1, first)
                    if g == 1 and not first:
                        upto_c(c + 1)
                        copy_y(i - 1, spot("w2", NG - 1))
                    upto_c(min(c + 2, PER_ITEM - 1))
                    act.wait_ge(used, i * PER_ITEM + (NW + c + 1))
                    act.activation(hs[g], ps[:, g % 2, :], ACT.Silu).then_inc(m_silu, 1)
                    if g:
                        hidden_hi(i, g - 1)
                    elif not first:
                        hidden_hi(i - 1, NG - 1)
                    if g == 3:
                        act.wait_ge(m_gt, i + 1)
                        act.activation(r4[:, 512:512 + SEQ], ps[:, 7, 0:SEQ], ACT.Copy).then_inc(m_gtc, 1)
                    if ahead and g >= NG - 2:
                        upto_c(min(c + 3, PER_ITEM - 1))
                        gather_hi(i + 1, 1 - par, g - (NG - 2))
                upto_c(PER_ITEM - 1)

            def drain(i):
                hidden_hi(i, NG - 1)
                copy_y(i, PER_ITEM - 1)

            item(0, 0, True, True)
            with act.Fori(0, EXPERTS // 2 - 1) as j:
                item(j * 2 + 1, 1, False, True)
                item(j * 2 + 2, 0, False, True)
            item(EXPERTS - 1, 1, False, False)
            drain(EXPERTS - 1)
            act.wait_ge(route_ready, 1)
            spare = act.value_load(info[0:1, ITEMS:ITEMS + 1], min_val=0, max_val=SPARE)
            with act.If(spare > 0):
                with act.Fori(EXPERTS, ITEMS) as i:
                    with act.If(i < spare + EXPERTS):
                        item(i, 0, True, False)
                        drain(i)
            act.activation(warm[:, :], warm[:, :], ACT.Sqrt)
            act.wait_ge(sum_ready, 1)
            for t in range(T):
                square(y_exp[:, t, :].rearrange("p (c s) -> p c s", c=2), t, t)
                root(1, t)

        @block.vector
        def _(dve):
            steps = [0]

            def link(ins):
                steps[0] += 1
                ins.then_inc(v_step, 1)
                dve.wait_ge(v_step, steps[0])

            done, sums, gates = [0], [0], [0]

            def acc_of(a):
                return r5 if a == 1 else acc

            def ada_quarter(a, q):
                l, v = ADA[a]
                ac = acc_of(a)
                r = RAW_OF["ada", a, q]
                dve.wait_ge(raw_full[r % NRAW], 16 * (r // NRAW + 1))
                if q == 0 and a > 1:
                    dve.wait_ge(ada_full, sum(2 if ADA[b][1] in (G_M, G_F) else 1 for b in range(a)))
                for kk in range(2):
                    w = raw[:, r % NRAW, kk * D:(kk + 1) * D]
                    c = cact[:, 2 * q + kk:2 * q + kk + 1]
                    if q == 0 and kk == 0:
                        link(dve.tensor_scalar(ac[:, :], w, c, None, ALU.mult))
                    else:
                        m = dve.scalar_tensor_tensor(ac[:, :], w, c, ac[:, :], ALU.mult, ALU.add)
                        if kk == 0:
                            link(m)
                m.then_inc(raw_done, 1)
                dve.wait_ge(raw_done, r + 1)
                if q == 3 and v in (G_M, G_F):
                    for k in range(K):
                        m = dve.scalar_tensor_tensor(ac[:, k * P:(k + 1) * P], ident[:, :], col(COL_ADA + (l * 6 + v) * K + k),
                                                     ac[:, k * P:(k + 1) * P], ALU.mult, ALU.add)
                    m.then_inc(ada_acc, 1)
                    gates[0] += 1
                    dve.wait_ge(ada_acc, gates[0])

            def ada_use(a, half):
                l, v = ADA[a]
                sums[0] += 1
                dve.wait_ge(ada_full, sums[0])
                n = 2 * l + (v >= SH_F)
                if v in (G_M, G_F):
                    gate, arrived = (gate_m, post_m_in) if v == G_M else (gate_f, post_f_in)
                    dve.wait_ge(arrived, 16 * (l + 1))
                    g = gate[:, half * 512:(half + 1) * 512]
                    dve.tensor_tensor(g, ps[:, 7, :], g, ALU.mult).then_inc(ada_used, 1)
                    dve.wait_ge(ada_used, sums[0])
                    return
                bias = cols[:, COL_ADA + (l * 6 + v) * K:COL_ADA + (l * 6 + v + 1) * K]
                what = AB[:, n, 0 if v in (SC_M, SC_F) else 1, :]
                dve.tensor_tensor(what, ps[:, 7, 0:K], bias, ALU.add).then_inc(ada_used, 1)
                dve.wait_ge(ada_used, sums[0])
                if v in (SC_M, SC_F):
                    link(dve.scalar_tensor_tensor(what, what, 1.0, cols[:, COL_NORM + n * K:COL_NORM + (n + 1) * K], ALU.add, ALU.mult))

            def lo_part(s):
                r, e = RAW_OF["w", s, 0], WEIGHTS[s][3]
                dve.wait_ge(hi_done, s + 1)
                dve.tensor_tensor(lo[:, s % NSPLIT, 0:e], raw[:, r % NRAW, 0:e], hi[:, s % NSPLIT, 0:e].bitcast(f32),
                                  ALU.subtract).then_inc(raw_done, 1)

            def upto(name, ahead=2):
                while done[0] < min(CHUNK[name] + ahead + 1, NW):
                    s = done[0]
                    for a, (_, _, at) in enumerate(ADA_AT, len(ADA_FIRST)):
                        if at <= s < at + 4:
                            ada_quarter(a, s - at)
                    lo_part(s)
                    for a, half, _, use in SUMS:
                        if use == s:
                            ada_use(a, half)
                    done[0] += 1

            roots = [0]

            def root(n):
                link(dve.tensor_scalar(ms[:, 0:n], ms[:, 0:n], EPS, None, ALU.add))
                dve.reciprocal(ms[:, 0:n], ms[:, 0:n]).then_inc(var_ready, 1)
                roots[0] += 1
                dve.wait_ge(rstd_ready, roots[0])

            def mean_square(src, scratch, at, width):
                return dve.scalar_tensor_tensor(scratch, src, 1.0 / width, src, ALU.mult, ALU.mult, accum_out=ms[:, at:at + 1])

            def item_lo(i, lo_c, hi_c):
                for c in range(lo_c, hi_c):
                    slot, s = (NR + c) % NRAW, (NW + c) % NSPLIT
                    dve.wait_ge(hi_done, i * PER_ITEM + (NW + c + 1))
                    dve.tensor_tensor(lo[:, s, :], raw[:, slot, :], hi[:, s, :].bitcast(f32), ALU.subtract).then_inc(raw_done, 1)

            squares = [0]

            def inverse(at):
                squares[0] += 1
                dve.wait_ge(sq_done, squares[0])
                link(dve.tensor_scalar(ms[:, at:at + 1], ms[:, at:at + 1], EPS, None, ALU.add))
                dve.reciprocal(ms[:, at:at + 1], ms[:, at:at + 1]).then_inc(var_ready, 1)
                roots[0] += 1

            def diagonal(t):
                dve.tensor_scalar(diag[:, t, :], ident[:, :], rstd[:, T + t:T + t + 1], None, ALU.mult).then_inc(diag_ready, 1)

            def h_part(n):
                def full(b):
                    dve.wait_ge(xt_full, 4 * n + b + 1)
                    for k in (2 * b, 2 * b + 1):
                        m = dve.tensor_scalar(hf[:, k, :], ps[:, X_BANKS[n][b], (k % 2) * SEQ:(k % 2 + 1) * SEQ],
                                              AB[:, n, 0, k:k + 1], AB[:, n, 1, k:k + 1], ALU.mult, ALU.add)
                    m.then_inc(hf_ready, 1)

                def rest(b):
                    dve.wait_ge(hth_ready, 4 * n + b + 1)
                    dve.tensor_tensor(hTl[:, 2 * b:2 * b + 2, :], hf[:, 2 * b:2 * b + 2, :],
                                      hTh[:, 2 * b:2 * b + 2, :].bitcast(f32), ALU.subtract).then_inc(ht_ready, 1)

                full(0)
                for b in range(1, 4):
                    full(b)
                    rest(b - 1)
                rest(3)

            def post(n, y, gate, following):
                for t in range(T):
                    inverse(t)
                    link(dve.tensor_tensor(y_sb[:, t, :].rearrange("p (c s) -> p c s", c=2), y[t],
                                           gate[:, :].rearrange("p (c s) -> p c s", c=2), ALU.mult))
                    if t and following:
                        dve.wait_ge(rstd_ready, roots[0])
                        inverse(T)
                        residual(n, t)
                        dve.wait_ge(rstd_ready, roots[0])
                        diagonal(0)
                        inverse(T + 1)
                        dve.wait_ge(rstd_ready, roots[0])
                        diagonal(1)
                    else:
                        dve.wait_ge(rstd_ready, roots[0])
                        residual(n, t)

            def residual(n, t):
                dve.scalar_tensor_tensor(x[:, t, :], y_sb[:, t, :], rstd[:, t:t + 1], x[:, t, :], ALU.mult, ALU.add).then_inc(x_done, 1)
                dve.wait_ge(x_done, T * n + t + 1)

            def in_psum(n):
                return [ps[:, b:b + 2, :] for b in Y_BANK[n]]

            dve.wait_ge(consts_in, 16)
            dve.wait_ge(cact_ready, 1)
            for q in range(4):
                ada_quarter(0, q)
            for q in range(4):
                ada_quarter(1, q)
                if q == 1:
                    ada_use(0, 0)
                    dve.wait_ge(pool_setup, 6)
                    for t in range(T):
                        inverse(T + t)
                        dve.wait_ge(rstd_ready, roots[0])
                        diagonal(t)
            upto("m0.cq0", 0)
            ada_use(1, 0)

            def mixer(l):
                h_part(2 * l)
                upto(f"m{l}.kr1")
                dve.wait_ge(lat_copied, 4 * l + 4)
                for t in range(T):
                    mean_square(lat[:, t, 0:QR], r6[:, t * QR:(t + 1) * QR], t, QR)
                for t in range(T):
                    m = mean_square(lat[:, t, QR:], r6[:, T * QR + t * KVR:T * QR + (t + 1) * KVR], T + t, KVR)
                link(m)
                root(2 * T)
                for t in range(T):
                    dve.tensor_scalar(lat[:, t, 0:QR], lat[:, t, 0:QR], rstd[:, t:t + 1], None, ALU.mult)
                    m = dve.tensor_scalar(lat[:, t, QR:], lat[:, t, QR:], rstd[:, T + t:T + t + 1], None, ALU.mult)
                m.then_inc(lat_ready, 1)
                upto(f"m{l}.v1")
                for kk in range(LATC):
                    dve.wait_ge(latTh_ready, LATC * l + min(kk - kk % 2 + 2, LATC))
                    at = COL_QN + l * QC + kk if kk < QC else COL_KVN + l * KC + kk - QC
                    dve.scalar_tensor_tensor(bTl[:, kk, :], ps[:, [5, 6, 0][kk // 2], (kk % 2) * SEQ:(kk % 2 + 1) * SEQ],
                                             col(at), bTh[:, kk, :].bitcast(f32), ALU.mult, ALU.subtract).then_inc(latT_ready, 1)
                dve.wait_ge(vu_done, 4 * l + 2)
                for t in range(T):
                    m = dve.bn_stats(bn[:, t, :], v_g[:, t, :])
                link(m)
                for t in range(T):
                    m = dve.bn_aggr(mv[:, t, :], bn[:, t, :])
                link(m)
                link(dve.tensor_copy(ms[:, 0:T], mv[:, :, 1]))
                root(T)
                for t in range(T):
                    m = dve.tensor_scalar(v_g[:, t, :], v_g[:, t, :], mv[:, t, 0:1], rstd[:, t:t + 1], ALU.subtract, ALU.mult)
                link(m)
                dve.wait_ge(ln_in, 32 * (l + 1))
                for t in range(T):
                    m = dve.tensor_tensor(v_g[:, t, :], v_g[:, t, :], ln_g, ALU.mult)
                link(m)
                for t in range(T):
                    m = dve.tensor_tensor(v_g[:, t, :], v_g[:, t, :], ln_b, ALU.add)
                m.then_inc(vn_ready, 1)
                dve.wait_ge(vn_ready, l + 1)
                upto(f"m{l}.ukv", 0)
                dve.wait_ge(rope_ready, 1)
                dve.wait_ge(attn_copied, 8 * l + 4)
                shape = [P, T, HEADS + 1, HALF]
                x1, x2 = qk[:, :, :, NOPE:NOPE + HALF], qk[:, :, :, NOPE + HALF:QKD]
                cb, sbc = (z[:, :, :].unsqueeze(2).to_broadcast(shape) for z in (cosT, sinT))
                n = T * (HEADS + 1) * HALF
                t0, t1 = (r6[:, i * n:(i + 1) * n].rearrange("p (t h d) -> p t h d", t=T, h=HEADS + 1) for i in range(2))
                dve.tensor_tensor(t0, x1, sbc, ALU.mult)
                link(dve.tensor_tensor(t1, x2, sbc, ALU.mult))
                dve.tensor_tensor(x1, x1, cb, ALU.mult)
                link(dve.tensor_tensor(x2, x2, cb, ALU.mult))
                dve.tensor_tensor(x1, x1, t1, ALU.subtract)
                link(dve.tensor_tensor(x2, x2, t0, ALU.add))
                for t in range(T):
                    m = dve.tensor_copy(k_tok[:, t, :, NOPE:QKD],
                                        qk[:, t, HEADS, NOPE:QKD].unsqueeze(1).to_broadcast([P, HEADS, ROPE]))
                m.then_inc(qk_ready, 1)
                upto(f"m{l}.ukv", 1)
                for j in range(4):
                    dve.wait_ge(kT_full, 4 * l + j + 1)
                    dve.tensor_copy(kT[:, 2 * j:2 * j + 2, :], ps[0:QKD, 3 + j, :].rearrange("p (h s) -> p h s", h=2)).then_inc(kT_copied, 1)
                dve.wait_ge(vu_done, 4 * l + 4)
                for t in range(T):
                    dve.wait_ge(z_full, T * l + t + 1)
                    for g in range(GROUPS):
                        u = u_g[:, t, g * GDIM:(g + 1) * GDIM]
                        m = dve.scalar_tensor_tensor(u, ps[:, t, g * GDIM:(g + 1) * GDIM], col(COL_BS + l * GROUPS + g), u, ALU.add, ALU.mult)
                    m.then_inc(uz_ready, 1)
                for u in range(6):
                    heads, keys = (4, P) if u < 2 else (2, SEQ)
                    dve.wait_ge(sc_full, 6 * l + u + 1)
                    if u >= 4:
                        dve.wait_ge(pT_full, 6 * l + u - 3)
                    sv = S[:, u % 4, :].rearrange("p (h s) -> p h s", h=heads)
                    mb = mask[:, 2 * P - keys:2 * P].unsqueeze(1).to_broadcast([P, heads, keys])
                    dve.tensor_tensor(sv, ps[:, [2, 3, 4, 5, 6, 0][u], :].rearrange("p (h s) -> p h s", h=heads), mb, ALU.add).then_inc(s_ready, 1)
                    dve.wait_ge(s_ready, 6 * l + u + 1)
                    link(dve.reduce_max(mx[:, u, 0:heads], sv, AX))
                    dve.tensor_scalar(nmx[:, u, 0:heads], mx[:, u, 0:heads], -(QKD ** -0.5), None, ALU.mult).then_inc(nmx_ready, 1)
                upto(f"m{l}.ukv")
                for t in range(T):
                    dve.wait_ge(p_ready, 6 * l + (2, 6)[t])
                    if t == 0:
                        src, dst = psum_p[:, 0:2, 0:4], rinv[:, 0, :].rearrange("p (a b) -> p a b", a=2)
                    else:
                        src, dst = psum_p[:, 2:6, 0:2], rinv[:, 1, :].rearrange("p (a b) -> p a b", a=4)
                    link(dve.reciprocal(dst, src))
                    dve.wait_ge(o_full, T * l + t + 1)
                    dve.tensor_tensor(o_tok[:, t, :].rearrange("p (h d) -> p h d", h=HEADS), ps[:, 2 + t, :].rearrange("p (h d) -> p h d", h=HEADS),
                                      rinv[:, t, :].unsqueeze(2).to_broadcast([P, HEADS, VD]), ALU.mult).then_inc(o_ready, 1)
                for i in range(2 * T):
                    t = i % T
                    dve.wait_ge(brTh_ready, 4 * l + i + 1)
                    dst = slice(4 * (i // T), 4 * (i // T) + 4), slice(t * P, (t + 1) * P)
                    dve.tensor_tensor(bTl[:, dst[0], dst[1]], ps[:, [4, 5, 6, 0][i], :].rearrange("p (c s) -> p c s", c=4),
                                      bTh[:, dst[0], dst[1]].bitcast(f32), ALU.subtract).then_inc(brT_ready, 1)
                def merged_lo(h):
                    dve.wait_ge(mth_ready, 2 * l + h + 1)
                    dve.tensor_tensor(hTl[:, 4 * h:4 * h + 4, :], merged[:, 4 * h:4 * h + 4, :],
                                      hTh[:, 4 * h:4 * h + 4, :].bitcast(f32), ALU.subtract).then_inc(mt_ready, 1)

                for j in range(4):
                    upto(f"m{l}.ab{j}")
                    if j == 3:
                        merged_lo(0)
                    dve.wait_ge(used, CHUNK[f"m{l}.ab{j}"] + 1)
                    for m_ in range(2):
                        mm = 2 * j + m_
                        sg = S[:, mm % 4, :]
                        dve.wait_ge(sig_done, 8 * l + mm + 1)
                        link(dve.tensor_tensor(sg, sg, ps[:, [3, 5][j % 2] + m_, :], ALU.mult))
                        dve.tensor_tensor(merged[:, mm, :], sg[:, 0:SEQ], sg[:, SEQ:2 * SEQ], ALU.add).then_inc(mg_done, 1)
                merged_lo(1)
                upto(f"m{l}.wo3")
                if l == L - 1:
                    item_lo(0, 0, 2)
                post(2 * l, in_psum(2 * l), gate_m, True)

            def ffn():
                h_part(1)
                for j in range(FG):
                    upto(f"fu{j}")
                    for i in (2 * j, 2 * j + 1):
                        a = r4[:, (i % 4) * SEQ:(i % 4 + 1) * SEQ]
                        dve.wait_ge(silu_done, i + 1)
                        dve.tensor_tensor(a, a, ps[:, i % 3, SEQ:2 * SEQ], ALU.mult).then_inc(hb_done, 1)
                    for i in (2 * j, 2 * j + 1):
                        dve.wait_ge(hbh_ready, i + 1)
                        dve.tensor_tensor(bTl[:, i % K, :], r4[:, (i % 4) * SEQ:(i % 4 + 1) * SEQ], bTh[:, i % K, :].bitcast(f32),
                                          ALU.subtract).then_inc(hb_ready, 1)
                upto(f"fd{FG - 1}")
                post(1, in_psum(1), gate_f, True)

            mixer(0)
            ffn()
            mixer(1)
            h_part(3)

            E = EXPERTS
            at = [0]

            def tile(*shape):
                n = int(np.prod(shape))
                v = r4[:, 1024 + at[0]:1024 + at[0] + n]
                at[0] += n
                return v.rearrange("p (a b) -> p a b", a=shape[0]) if len(shape) == 2 else (
                    v.rearrange("p (a b c) -> p a b c", a=shape[0], b=shape[1]) if len(shape) == 3 else v)

            ex, sel, lg, rank = tile(T, E), tile(T, E), tile(T, E), tile(T, E)
            cmp, eq = tile(T, E, E), tile(T, E, E)
            ov, orank, ee, one, which, w3 = tile(E), tile(E), tile(E, E), tile(SPARE, E), tile(SPARE, E), tile(T, SPARE, E)
            info_f = tile(ITEMS + 1)
            for t in range(T):
                dve.wait_ge(router_full, t + 1)
                m = dve.tensor_tensor(lg[:, t, :], ps[:, R_BANK[t], 0:E], rb[:, :], ALU.add)
            link(m)
            for t in range(T):
                other = lg[:, t, :].unsqueeze(1).to_broadcast([P, E, E])
                own = lg[:, t, :].unsqueeze(2).to_broadcast([P, E, E])
                dve.tensor_tensor(cmp[:, t], other, own, ALU.is_gt)
                m = dve.tensor_tensor(eq[:, t], other, own, ALU.is_equal)
            link(m)
            for t in range(T):
                m = dve.tensor_tensor(eq[:, t], eq[:, t], lt_mask[:, :, :], ALU.mult)
            link(m)
            link(dve.tensor_tensor(cmp, cmp, eq, ALU.add))
            link(dve.reduce_sum(rank, cmp, AX))
            dve.tensor_scalar(sel, rank, 1.5, None, ALU.is_lt).then_inc(sel_ready, 1)
            dve.wait_ge(sel_ready, 1)
            link(dve.reduce_max(small[:, 0:T], lg, AX))
            for t in range(T):
                m = dve.tensor_scalar(ex[:, t, :], lg[:, t, :], small[:, t:t + 1], None, ALU.subtract)
            m.then_inc(ex_in, 1)
            dve.wait_ge(count_full, 1)
            slot = pos_tab[:, :, 0:E]
            link(dve.scalar_tensor_tensor(slot, ps[:, 7, 32:32 + T * E].rearrange("p (t e) -> p t e", t=T), 1.0, sel, ALU.add, ALU.mult))
            dve.tensor_scalar(slot, slot, -1.0, None, ALU.add).then_inc(pos_ready, 1)
            dve.wait_ge(pos_ready, 1)

            def gates():
                dve.wait_ge(ex_done, 1)
                link(dve.tensor_tensor(ex, ex, sel, ALU.mult))
                link(dve.reduce_sum(small[:, T:2 * T], ex, AX))
                link(dve.reciprocal(small[:, T:2 * T], small[:, T:2 * T]))
                for t in range(T):
                    m = dve.tensor_scalar(gate_tab[:, t, 0:E], ex[:, t, :], small[:, T + t:T + t + 1], None, ALU.mult)
                m.then_inc(gates_ready, 1)
                dve.wait_ge(gates_ready, 1)

            def spares():
                dve.wait_ge(count_full, 2)
                link(dve.tensor_scalar(ov, ps[:, R_BANK[1], 32:32 + E], P + 0.5, None, ALU.is_gt))
                dve.memset(info_f[:, 0:ITEMS], 0.0)
                link(dve.reduce_sum(info_f[:, ITEMS:ITEMS + 1], ov, AX))
                link(dve.tensor_tensor(ee, lt_mask[:, :, :], ov.unsqueeze(1).to_broadcast([P, E, E]), ALU.mult))
                link(dve.reduce_sum(orank, ee, AX))
                link(dve.tensor_tensor(one, spare_no[:, :, :], orank.unsqueeze(1).to_broadcast([P, SPARE, E]), ALU.is_equal))
                link(dve.tensor_tensor(one, one, ov.unsqueeze(1).to_broadcast([P, SPARE, E]), ALU.mult))
                link(dve.tensor_tensor(which, one, eidx[:, :].unsqueeze(1).to_broadcast([P, SPARE, E]), ALU.mult))
                dve.reduce_sum(info_f[:, E:ITEMS], which, AX)
                for t in range(T):
                    m = dve.scalar_tensor_tensor(w3[:, t], pos_tab[:, t, 0:E].unsqueeze(1).to_broadcast([P, SPARE, E]), 1.0 - P,
                                                 one, ALU.add, ALU.mult)
                link(m)
                link(dve.reduce_sum(pos_tab[:, :, E:ITEMS], w3, AX))
                link(dve.tensor_scalar(pos_tab[:, :, E:ITEMS], pos_tab[:, :, E:ITEMS], -1.0, None, ALU.add))
                for t in range(T):
                    m = dve.tensor_tensor(w3[:, t], gate_tab[:, t, 0:E].unsqueeze(1).to_broadcast([P, SPARE, E]), one, ALU.mult)
                link(m)
                link(dve.reduce_sum(gate_tab[:, :, E:ITEMS], w3, AX))
                dve.tensor_copy(info[:, :], info_f).then_inc(route_ready, 1)
                dve.wait_ge(route_ready, 1)

            def one_hot(t, value):
                return dve.tensor_scalar(r4[:, t * P:(t + 1) * P], slots[:, :], pg[:, 0, t:t + 1], value, ALU.is_equal, ALU.mult)

            def gate_hot(t):
                return dve.tensor_scalar(r4[:, 256 + t * P:256 + (t + 1) * P], slots[:, :], pg[:, 0, t:t + 1], pg[:, 1, t:t + 1],
                                         ALU.is_equal, ALU.mult)

            def select(i):
                dve.tensor_copy(pg[:, 0, :], pos_tab[:, :, bass.ds(i, 1)].rearrange("p t o -> p (t o)"))
                dve.tensor_copy(pg[:, 1, :], gate_tab[:, :, bass.ds(i, 1)].rearrange("p t o -> p (t o)")).then_inc(v_loop, 1)
                dve.wait_ge(v_loop, i + 1)
                for t in range(T):
                    one_hot(t, rstd[:, T + t:T + t + 1])
                    m = gate_hot(t)
                m.then_inc(m_pos, 1)

            def select_first():
                link(dve.tensor_copy(pg[:, 0, :], pos_tab[:, :, 0]))
                for t in range(T):
                    m = one_hot(t, rstd[:, T + t:T + t + 1])
                m.then_inc(m_pos, 1)
                gates()
                dve.tensor_copy(pg[:, 1, :], gate_tab[:, :, 0]).then_inc(v_loop, 1)
                dve.wait_ge(v_loop, 1)
                for t in range(T):
                    m = gate_hot(t)
                m.then_inc(gates_ready, 1)

            def gathered(i, h, first):
                dve.wait_ge(m_gath, i * 2 + h + 1)
                bank = 6 if first and h else 7
                for kk in range(4):
                    k = 4 * h + kk
                    m = dve.tensor_scalar(r3[:, k * P:(k + 1) * P], ps[:, bank, kk * P:(kk + 1) * P],
                                          AB[:, 3, 0, k:k + 1], AB[:, 3, 1, k:k + 1], ALU.mult, ALU.add)
                m.then_inc(m_xf, 1)

            def gathered_lo(i, par, h):
                dve.wait_ge(m_xh, i * 2 + h + 1)
                at = slice(par * P, (par + 1) * P)
                dve.tensor_tensor(hTl[:, 4 * h:4 * h + 4, at], r3[:, 512 * h:512 * h + 512].rearrange("p (k s) -> p k s", k=4),
                                  hTh[:, 4 * h:4 * h + 4, at].bitcast(f32), ALU.subtract).then_inc(m_x, 1)

            def hidden(i, g, first):
                a = hs[g]
                dve.wait_ge(m_silu, i * NG + g + 1)
                dve.wait_ge(used, i * PER_ITEM + (NW + spot("w3", g, 1, first) + 1))
                dve.tensor_tensor(a, a, ps[:, 2 + g % 2, :], ALU.mult).then_inc(m_hb, 1)

            def hidden_lo(i, g):
                dve.wait_ge(m_hh, i * NG + g + 1)
                dve.tensor_tensor(bTl[:, 0:4, 0:P], ps[:, 6, :].rearrange("p (c s) -> p c s", c=4),
                                  bTh[:, 0:4, 0:P].bitcast(f32), ALU.subtract).then_inc(m_h, 1)

            def add_y(i, q, bank=7):
                ya = y_exp[:, q // 2, (q % 2) * 512:(q % 2 + 1) * 512]
                if q == 0:
                    dve.wait_ge(m_acc, i * 4 + 1)
                dve.wait_ge(m_sc, i * 4 + q + 1)
                dve.tensor_tensor(ya, ya, ps[:, bank, :], ALU.add).then_inc(m_acc, 1)

            def item(i, par, first, ahead):
                if first:
                    if ahead:
                        select_first()
                        item_lo(0, 2, 3)
                    else:
                        dve.wait_ge(m_gt, i)
                        select(i)
                    for h in range(2):
                        gathered(i, h, True)
                        gathered_lo(i, par, h)
                    if ahead:
                        spares()
                    else:
                        item_lo(i, 0, 2)
                at = [(3 if ahead else 2) if first else 0]

                def upto_c(c):
                    item_lo(i, at[0], c + 1)
                    at[0] = max(at[0], c + 1)

                for g in range(NG):
                    upto_c(spot("w1", g, 1, first) + 2)
                    if g:
                        hidden_lo(i, g - 1)
                    elif not first:
                        hidden_lo(i - 1, NG - 1)
                    if not first and g in (1, 2):
                        add_y(i - 1, 2 * g - 2)
                    if ahead and g == 4:
                        dve.wait_ge(m_gt, i + 1)
                        select(i + 1)
                    if ahead and g >= NG - 2:
                        gathered(i + 1, g - (NG - 2), False)
                    upto_c(spot("w3", g, 1, first) + 2)
                    hidden(i, g, first)
                    if not first and g in (1, 2):
                        add_y(i - 1, 2 * g - 1)
                    if ahead and g >= NG - 2:
                        gathered_lo(i + 1, 1 - par, g - (NG - 2))
                upto_c(PER_ITEM - 1)

            def drain(i):
                hidden_lo(i, NG - 1)
                for q in range(4):
                    add_y(i, q, DRAIN[q])
                dve.wait_ge(m_acc, i * 4 + 5)
                dve.memset(small[:, 0:1], 0.0)

            item(0, 0, True, True)
            with dve.Fori(0, EXPERTS // 2 - 1) as j:
                item(j * 2 + 1, 1, False, True)
                item(j * 2 + 2, 0, False, True)
            item(EXPERTS - 1, 1, False, False)
            drain(EXPERTS - 1)
            spare = dve.value_load(info[0:1, ITEMS:ITEMS + 1], min_val=0, max_val=SPARE)
            with dve.If(spare > 0):
                with dve.Fori(EXPERTS, ITEMS) as i:
                    with dve.If(i < spare + EXPERTS):
                        item(i, 0, True, False)
                        drain(i)
            dve.memset(small[:, 1:2], 0.0).then_inc(sum_ready, 1)
            post(3, [y_exp[:, t, :].rearrange("p (c s) -> p c s", c=2) for t in range(T)], gate_f, False)

        @block.tensor
        def _(pe):
            summed, gates = [0], [0]

            def three(o, wh, wl, mh, ml, first, last):
                pe.matmul(o, wh, mh, start=first, stop=False)
                pe.matmul(o, wh, ml, start=False, stop=False)
                return pe.matmul(o, wl, mh, start=False, stop=last)

            def ada_sum(a, half):
                l, v = ADA[a]
                if v in (G_M, G_F):
                    if half == 0:
                        gates[0] += 1
                    pe.wait_ge(ada_acc, gates[0])
                else:
                    pe.wait_ge(raw_done, RAW_OF["ada", a, 3] + 1)
                if summed[0]:
                    pe.wait_ge(ada_used, summed[0])
                if v in (G_M, G_F):
                    m = pe.matmul(ps[:, 7, :], ones[:, :], acc[:, half * 512:(half + 1) * 512], start=True, stop=True)
                else:
                    for k in range(K):
                        m = pe.matmul(ps[:, 7, k:k + 1], (r5 if a == 1 else acc)[:, k * P:(k + 1) * P], ones[:, 0:1], start=True, stop=True)
                m.then_inc(ada_full, 1)
                summed[0] += 1

            def chunk(name):
                s = CHUNK[name]
                pe.wait_ge(raw_done, RAW_OF["w", s, 0] + 1)
                return hi[:, s % NSPLIT, :], lo[:, s % NSPLIT, :]

            def finish(name, m):
                m.then_inc(used, 1)
                for a, half, after, _ in SUMS:
                    if after == CHUNK[name]:
                        ada_sum(a, half)

            def h_turn(n):
                for t in range(T):
                    pe.wait_ge(diag_ready, T * n + t + 1)
                    for k in range(K):
                        m = pe.matmul(ps[:, X_BANKS[n][k // 2], (k % 2) * SEQ + t * P:(k % 2) * SEQ + (t + 1) * P],
                                      x[:, t, k * P:(k + 1) * P], diag[:, t, :], start=True, stop=True)
                        if t == T - 1 and k % 2:
                            m.then_inc(xt_full, 1)

            def by_token(name, l, width, banks):
                for h in range(2):
                    wh, wl = chunk(f"m{l}.{name}{h}")
                    for t in range(T):
                        for kk in range(4):
                            k = 4 * h + kk
                            if name == "cq" and t == 0 and k % 2 == 0:
                                pe.wait_ge(ht_ready, 8 * l + k // 2 + 1)
                            w = slice(kk * width, (kk + 1) * width)
                            m = three(ps[:, banks[t], 0:width], hTh[:, k, t * P:(t + 1) * P], hTl[:, k, t * P:(t + 1) * P],
                                      wh[:, w], wl[:, w], k == 0, k == K - 1)
                    finish(f"m{l}.{name}{h}", m)

            pe.wait_ge(pool_setup, 6)
            ada_sum(0, 0)

            def mixer(l):
                h_turn(2 * l)
                if l == 0:
                    ada_sum(1, 0)
                by_token("cq", l, QR, (4, 5))
                by_token("kr", l, KVR + ROPE, (6, 0))
                by_token("v", l, GW, (1, 2))
                pe.wait_ge(lat_ready, l + 1)
                for kk in range(LATC):
                    for t in range(T):
                        m = pe.transpose(ps[:, [5, 6, 0][kk // 2], (kk % 2) * SEQ + t * P:(kk % 2) * SEQ + (t + 1) * P],
                                         lat[:, t, kk * P:(kk + 1) * P], ident[:, :])
                    if kk % 2 or kk == LATC - 1:
                        m.then_inc(latT_full, 1)
                by_token("u", l, GW, (3, 4))
                pe.wait_ge(latT_ready, LATC * (l + 1))
                for h in range(2):
                    wh, wl = chunk(f"m{l}.uq{h}")
                    for t in range(T):
                        if (h, t) == (1, 1):
                            pe.wait_ge(vu_done, 4 * l + 1)
                        for kk in range(QC):
                            w = slice(kk * QR, (kk + 1) * QR)
                            m = three(ps[:, [5, 6, 0, 1][2 * h + t], 0:QR], bTh[:, kk, t * P:(t + 1) * P], bTl[:, kk, t * P:(t + 1) * P],
                                      wh[:, w], wl[:, w], kk == 0, kk == QC - 1)
                    finish(f"m{l}.uq{h}", m)
                wh, wl = chunk(f"m{l}.ukv")
                for half in range(2):
                    for t in range(T):
                        i = 2 * half + t
                        if i < 3:
                            pe.wait_ge(vu_done, 4 * l + 2 + i)
                        else:
                            pe.wait_ge(attn_copied, 8 * l + 1)
                        for kk in range(KC):
                            w = slice(kk * D + half * 512, kk * D + (half + 1) * 512)
                            m = three(ps[:, 2 + i, :], bTh[:, QC + kk, t * P:(t + 1) * P], bTl[:, QC + kk, t * P:(t + 1) * P],
                                      wh[:, w], wl[:, w], kk == 0, kk == KC - 1)
                finish(f"m{l}.ukv", m)
                pe.wait_ge(attn_copied, 8 * l + 8)
                pe.wait_ge(qk_ready, l + 1)
                for j in range(4):
                    for hh in range(2):
                        for t in range(T):
                            m = pe.transpose(ps[0:QKD, [6, 0, 1, 2][j], hh * SEQ + t * P:hh * SEQ + (t + 1) * P],
                                             qk[:, t, 2 * j + hh, :], ident[:, :])
                    m.then_inc(qT_full, 1)
                for j in range(4):
                    if j == 3:
                        pe.wait_ge(qT_copied, 4 * l + 1)
                    for hh in range(2):
                        for t in range(T):
                            m = pe.transpose(ps[0:QKD, 3 + j, hh * SEQ + t * P:hh * SEQ + (t + 1) * P],
                                             k_tok[:, t, 2 * j + hh, :], ident[:, :])
                    m.then_inc(kT_full, 1)
                pe.wait_ge(vn_ready, l + 1)
                pe.wait_ge(ws_masked, l + 1)
                for t in range(T):
                    pe.wait_ge(qT_copied, 4 * l + 2 + t)
                    for g in range(GROUPS):
                        m = pe.matmul(ps[:, t, g * GDIM:(g + 1) * GDIM], ws[:, g, :], v_g[:, t, g * GDIM:(g + 1) * GDIM],
                                      start=True, stop=True)
                    m.then_inc(z_full, 1)
                pe.wait_ge(qT_copied, 4 * l + 4)
                pe.wait_ge(kT_copied, 4 * l + 4)
                for u in range(6):
                    t, heads = (0, range(4 * u, 4 * u + 4)) if u < 2 else (1, (2 * u - 4, 2 * u - 3))
                    keys = (t + 1) * P
                    if u == 5:
                        pe.wait_ge(uz_ready, T * l + 1)
                    for n, h in enumerate(heads):
                        m = pe.matmul(ps[:, [2, 3, 4, 5, 6, 0][u], n * keys:(n + 1) * keys], qT[:, h, t * P:(t + 1) * P],
                                      kT[:, h, 0:keys], start=True, stop=True)
                    m.then_inc(sc_full, 1)

                def turn_p(u):
                    if u == 0:
                        pe.wait_ge(uz_ready, T * l + 2)
                    pe.wait_ge(p_ready, 6 * l + u + 1)
                    for c in range(4):
                        m = pe.transpose(ps[:, 1 + u, c * P:(c + 1) * P], S[:, u % 4, c * P:(c + 1) * P], ident[:, :])
                    m.then_inc(pT_full, 1)

                def weigh_v(t):
                    pe.wait_ge(pT_copied, 6 * l + (2, 6)[t])
                    for h in range(HEADS):
                        for kb in range(t + 1):
                            slot, c = (h // 4, h % 4) if t == 0 else ((2 + h // 2) % 4, (h % 2) * 2 + kb)
                            m = pe.matmul(ps[:, 2 + t, h * VD:(h + 1) * VD], pT[:, slot, c * P:(c + 1) * P],
                                          v_tok[:, kb, h * VD:(h + 1) * VD], start=(kb == 0), stop=(kb == t))
                    m.then_inc(o_full, 1)

                for u in range(4):
                    turn_p(u)
                weigh_v(0)
                turn_p(4)
                turn_p(5)
                weigh_v(1)
                for i, src in enumerate((u_g, u_g, o_tok, o_tok)):
                    t = i % T
                    if i >= T:
                        pe.wait_ge(o_ready, T * l + t + 1)
                    for c in range(4):
                        m = pe.transpose(ps[:, [4, 5, 6, 0][i], c * P:(c + 1) * P], src[:, t, c * P:(c + 1) * P], ident[:, :])
                    m.then_inc(brT_full, 1)
                for j in range(4):
                    for half, name in enumerate((f"m{l}.ga{j}", f"m{l}.gb{j}")):
                        wh, wl = chunk(name)
                        for m_ in range(2):
                            if j and half == 0:
                                pe.wait_ge(sig_done, 8 * l + 2 * (j - 1) + m_ + 1)
                            for k in range(K):
                                w = slice(k * 2 * P + m_ * P, k * 2 * P + (m_ + 1) * P)
                                m = three(ps[:, 1 + m_, half * SEQ:(half + 1) * SEQ], wh[:, w], wl[:, w], hTh[:, k, :], hTl[:, k, :],
                                          k == 0, k == K - 1)
                        finish(name, m)
                    wh, wl = chunk(f"m{l}.ab{j}")
                    if j == 0:
                        pe.wait_ge(brT_ready, 4 * l + 4)
                    for m_ in range(2):
                        if j >= 2:
                            pe.wait_ge(mg_done, 8 * l + 2 * (j - 2) + m_ + 1)
                        for k in range(K):
                            w = slice(k * 2 * P + m_ * P, k * 2 * P + (m_ + 1) * P)
                            m = three(ps[:, [3, 5][j % 2] + m_, (k // 4) * SEQ:(k // 4 + 1) * SEQ], wh[:, w], wl[:, w], bTh[:, k, :], bTl[:, k, :],
                                      k % 4 == 0, k % 4 == 3)
                    finish(f"m{l}.ab{j}", m)
                for j in range(4):
                    wh, wl = chunk(f"m{l}.wo{j}")
                    pe.wait_ge(mt_ready, 2 * l + 1 + j // 2)
                    for t in range(T):
                        for half in range(2):
                            for kk in range(2):
                                k = 2 * j + kk
                                w = slice(kk * D + half * 512, kk * D + (half + 1) * 512)
                                m = three(ps[:, Y_BANK[2 * l][t] + half, :], hTh[:, k, t * P:(t + 1) * P], hTl[:, k, t * P:(t + 1) * P],
                                          wh[:, w], wl[:, w], k == 0, k == K - 1)
                        if j == 3 and t == 0:
                            m.then_inc(y_full, 1)
                    finish(f"m{l}.wo{j}", m)

            def ffn():
                h_turn(1)

                def down(j):
                    wh, wl = chunk(f"fd{j}")
                    pe.wait_ge(hb_ready, 2 * j + 2)
                    for t in range(T):
                        for half in range(2):
                            for i in (2 * j, 2 * j + 1):
                                rows = slice(LASTROW if i == FT - 1 else 0, P)
                                w = slice((i - 2 * j) * D + half * 512, (i - 2 * j) * D + (half + 1) * 512)
                                m = three(ps[:, Y_BANK[1][t] + half, :], bTh[rows, i % K, t * P:(t + 1) * P], bTl[rows, i % K, t * P:(t + 1) * P],
                                          wh[rows, w], wl[rows, w], i == 0, i == FT - 1)
                        if j == FG - 1 and t == 0:
                            m.then_inc(y_full, 1)
                    finish(f"fd{j}", m)

                for j in range(FG):
                    for half, name in enumerate((f"fg{j}", f"fu{j}")):
                        wh, wl = chunk(name)
                        for m_ in range(2):
                            i = 2 * j + m_
                            if half == 0 and i >= 3:
                                pe.wait_ge(hb_done, i - 2)
                            for k in range(K):
                                if i == 0 and half == 0 and k % 2 == 0:
                                    pe.wait_ge(ht_ready, 4 + k // 2 + 1)
                                w = slice(k * 2 * P + m_ * P, k * 2 * P + (m_ + 1) * P)
                                m = three(ps[:, i % 3, half * SEQ:(half + 1) * SEQ], wh[:, w], wl[:, w], hTh[:, k, :], hTl[:, k, :],
                                          k == 0, k == K - 1)
                        finish(name, m)
                    if j:
                        down(j - 1)
                down(FG - 1)

            mixer(0)
            ffn()
            mixer(1)

            h_turn(3)
            pe.wait_ge(ada_used, summed[0])
            for k in range(K):
                if k % 2 == 0:
                    pe.wait_ge(hf_ready, 12 + k // 2 + 1)
                for t in range(T):
                    m = pe.matmul(ps[:, R_BANK[t], 0:EXPERTS], hf[:, k, t * P:(t + 1) * P],
                                  col(COL_WR + k * EXPERTS, EXPERTS), start=(k == 0), stop=(k == K - 1))
                    if k == K - 1:
                        m.then_inc(router_full, 1)
            pe.wait_ge(sel_ready, 1)
            sel = r4[:, 1024 + T * EXPERTS:1024 + 2 * T * EXPERTS].rearrange("p (t e) -> p t e", t=T)
            for t in range(T):
                for s in range(t + 1):
                    m = pe.matmul(ps[:, 7, 32 + t * EXPERTS:32 + (t + 1) * EXPERTS], before[:, :] if s == t else ones[:, :], sel[:, s, :],
                                  start=(s == 0), stop=(s == t))
            m.then_inc(count_full, 1)
            for s in range(T):
                m = pe.matmul(ps[:, R_BANK[1], 32:32 + EXPERTS], ones[:, :], sel[:, s, :], start=(s == 0), stop=(s == T - 1))
            m.then_inc(count_full, 1)

            def gather(i, part, bank=7):
                for kk in range(4):
                    k = 4 * part + kk
                    for t in range(T):
                        m = pe.matmul(ps[:, bank, kk * P:(kk + 1) * P], x[:, t, k * P:(k + 1) * P], r4[:, t * P:(t + 1) * P],
                                      start=(t == 0), stop=(t == T - 1))
                m.then_inc(m_gath, 1)

            def item(i, par, first, ahead):
                def part(c):
                    pe.wait_ge(raw_done, i * PER_ITEM + (NR + c + 1))
                    return hi[:, (NW + c) % NSPLIT, :], lo[:, (NW + c) % NSPLIT, :]

                def up(kind, g):
                    for half in range(2):
                        if kind == "w1" and g == 0:
                            pe.wait_ge(m_x, i * 2 + half + 1)
                        wh, wl = part(spot(kind, g, half, first))
                        for kk in range(4):
                            k = 4 * half + kk
                            w = slice(kk * GRP, (kk + 1) * GRP)
                            at = slice(par * P, (par + 1) * P)
                            m = three(ps[:, (0 if kind == "w1" else 2) + g % 2, :], hTh[:, k, at], hTl[:, k, at],
                                      wh[:, w], wl[:, w], k == 0, k == K - 1)
                        m.then_inc(used, 1)

                if first:
                    pe.wait_ge(m_pos, i + 1)
                    pe.wait_ge(m_acc, i * 4 + 1)
                    if ahead:
                        pe.wait_ge(pos_ready, 1)
                        pe.wait_ge(ht_ready, 16)
                    gather(i, 0)
                    gather(i, 1, 6)
                else:
                    pe.wait_ge(m_silu, i * NG)
                for g in range(NG):
                    up("w1", g)
                    if g:
                        turn(i, g - 1)
                    elif not first:
                        turn(i - 1, NG - 1)
                    if g == 1 and not first:
                        pe.wait_ge(m_yc, i)
                        scatter(i - 1, 0)
                    if g == 3:
                        pe.wait_ge(m_acc, i * 4 + 1)
                        if first and ahead:
                            pe.wait_ge(m_xf, i * 2 + 1)
                            pe.wait_ge(gates_ready, 2)
                        for t in range(T):
                            m = pe.transpose(ps[:, 7, t * P:(t + 1) * P], r4[:, 256 + t * P:256 + (t + 1) * P], ident[:, :])
                        m.then_inc(m_gt, 1)
                    if ahead and g == NG - 2:
                        pe.wait_ge(m_gtc, i + 1)
                        pe.wait_ge(m_pos, i + 2)
                        gather(i + 1, 0)
                    if ahead and g == NG - 1:
                        pe.wait_ge(m_xf, i * 2 + 3)
                        gather(i + 1, 1)
                    if first and ahead and g == 0:
                        pe.wait_ge(route_ready, 1)
                    up("w3", g)
                    if g in (1, 2) and not first:
                        scatter(i - 1, 2 * g - 1)
                    if g:
                        down(i, g - 1, spot("w2", g - 1, 0))
                    elif not first:
                        down(i - 1, NG - 1, spot("w2", NG - 1, 0))
                    if g == 1 and not first:
                        scatter(i - 1, 2)

            def turn(i, g):
                pe.wait_ge(m_hb, i * NG + g + 1)
                for c in range(4):
                    m = pe.transpose(ps[:, 6, c * P:(c + 1) * P], hs[g][:, c * P:(c + 1) * P], ident[:, :])
                m.then_inc(m_t, 1)

            def down(i, g, c0):
                pe.wait_ge(m_h, i * NG + g + 1)
                for half in range(2):
                    n = c0 + half
                    pe.wait_ge(raw_done, i * PER_ITEM + (NR + n + 1))
                    wh, wl = hi[:, (NW + n) % NSPLIT, :], lo[:, (NW + n) % NSPLIT, :]
                    for cc in range(2):
                        c = 2 * half + cc
                        for q in range(2):
                            w = slice(cc * D + q * 512, cc * D + (q + 1) * 512)
                            m = three(ps[:, 4 + q, :], bTh[:, c, 0:P], bTl[:, c, 0:P], wh[:, w], wl[:, w],
                                      g == 0 and c == 0, g == NG - 1 and c == 3)
                    m.then_inc(used, 1)

            def scatter(i, q, bank=7):
                if q and bank == 7:
                    pe.wait_ge(m_acc, i * 4 + 1 + q)
                m = pe.matmul(ps[:, bank, :], r4[:, 512 + (q // 2) * P:512 + (q // 2 + 1) * P], r5[:, (q % 2) * 512:(q % 2 + 1) * 512],
                              start=True, stop=True)
                m.then_inc(m_sc, 1)

            def drain(i):
                turn(i, NG - 1)
                down(i, NG - 1, PER_ITEM - 2)
                pe.wait_ge(m_yc, i + 1)
                pe.wait_ge(m_gtc, i + 1)
                for q in range(4):
                    scatter(i, q, DRAIN[q])

            item(0, 0, True, True)
            with pe.Fori(0, EXPERTS // 2 - 1) as j:
                item(j * 2 + 1, 1, False, True)
                item(j * 2 + 2, 0, False, True)
            item(EXPERTS - 1, 1, False, False)
            drain(EXPERTS - 1)
            spare = pe.value_load(info[0:1, ITEMS:ITEMS + 1], min_val=0, max_val=SPARE)
            with pe.If(spare > 0):
                with pe.Fori(EXPERTS, ITEMS) as i:
                    with pe.If(i < spare + EXPERTS):
                        item(i, 0, True, False)
                        drain(i)


OUT_SHAPE = (1, SEQ, D)


def rows_of(w, kc, tiles=None):
    *lead, k, n = w.shape
    w = w.reshape(*lead, k // (kc * P), kc, P, n)
    return np.ascontiguousarray(np.swapaxes(w, -3, -2)).reshape(*lead, k // (kc * P), P, kc * n)


def cols_of(w, c):
    *lead, k, n = w.shape
    w = np.moveaxis(w.reshape(*lead, k // P, P, n // c, c), -2, -4)
    return np.ascontiguousarray(np.swapaxes(w, -3, -2)).reshape(*lead, n // c, P, k // P * c)


def channels(v):
    return np.moveaxis(v.reshape(*v.shape[:-1], v.shape[-1] // P, P), -1, 0).reshape(P, -1)


def lay_out(i):
    w_in = i["w_in"]
    u, v, cq, kr, ga, gb = np.split(w_in, np.cumsum([GW, GW, QR, KVR + ROPE, D]), axis=-1)
    ukv = i["mla_w_ukv"].reshape(L, KVR, HEADS, NOPE + VD)
    ukv = np.concatenate([ukv[..., :NOPE].reshape(L, KVR, -1), ukv[..., NOPE:].reshape(L, KVR, -1)], -1)
    cut = (FT - 1) * P
    wide = lambda w: np.concatenate([w[..., :cut], w[..., -P:]], -1)
    w_fd = i["ffn_w_down"]
    fd = np.concatenate([w_fd[:, :cut], w_fd[:, -P:]], 1)
    w_ada = i["ada_w"].reshape(L, 4, 2, P, 6, D).transpose(0, 4, 1, 3, 2, 5).reshape(L, 6, 4, P, CH)
    up = lambda w: np.ascontiguousarray(
        w[0].reshape(EXPERTS, 2, 4, P, NG, GRP).transpose(0, 4, 1, 3, 2, 5)).reshape(EXPERTS, NG, 2, P, CH)
    pack = np.concatenate([
        channels(i["c"]), channels(i["ada_b"]),
        channels(np.stack([i["norm_mix_pre"], i["norm_ffn_pre"]], 1)),
        channels(i["mla_q_norm"]), channels(i["mla_kv_norm"]),
        i["gmlp_bs"].transpose(2, 0, 1).reshape(P, -1),
        i["moe_router"][0].reshape(K, P, EXPERTS).transpose(1, 0, 2).reshape(P, -1)], 1)
    return {
        "x": i["x"], "cols": pack, "positions": i["positions"][0].reshape(T, P).T, "router_bias": i["moe_router_bias"],
        "ln_g": i["gmlp_ln_g"], "ln_b": i["gmlp_ln_b"], "post_m": i["norm_mix_post"], "post_f": i["norm_ffn_post"],
        "ws": i["gmlp_ws"].transpose(0, 3, 1, 2).reshape(L, P, GROUPS * P),
        "w_ada": w_ada, "w_cq": rows_of(cq, 4), "w_kr": rows_of(kr, 4), "w_v": rows_of(v, 4), "w_u": rows_of(u, 4),
        "w_uq": cols_of(i["mla_w_uq"], QR), "w_ukv": rows_of(ukv, KC),
        "w_ga": cols_of(ga, 2 * P), "w_gb": cols_of(gb, 2 * P),
        "w_ab": cols_of(np.concatenate([i["w_branch_a"], i["w_branch_b"]], 1), 2 * P), "w_o": rows_of(i["w_out"], 2),
        "w_fg": cols_of(wide(i["ffn_w_gate"]), 2 * P), "w_fu": cols_of(wide(i["ffn_w_up"]), 2 * P), "w_fd": rows_of(fd, 2),
        "moe_w1": up(i["moe_w1"]), "moe_w3": up(i["moe_w3"]),
        "moe_w2": rows_of(i["moe_w2"][0], 2).reshape(EXPERTS, NG, 2, P, CH),
    }


def kernel(**inputs):
    import concourse.bacc as _bacc
    from concourse.bass_utils import run_bass_kernel_spmd as _run

    nc = _bacc.Bacc("TRN2", target_bir_lowering=False, num_devices=1)
    arrays, args = {}, {}
    for name, a in lay_out({k: np.asarray(v) for k, v in inputs.items()}).items():
        a = np.ascontiguousarray(a)
        arrays[f"in_{name}_dram"] = a
        args[name] = nc.dram_tensor(f"in_{name}_dram", a.shape, mybir.dt.from_np(a.dtype), kind="ExternalInput").ap()
    out = nc.dram_tensor("out_0_dram", OUT_SHAPE, f32, kind="ExternalOutput").ap()
    build(nc, args, out)
    r = _run(nc, [arrays], core_ids=[0])
    return r.results[0]["out_0_dram"]
```
